# Optimizing a Trainium2 kernel written in Bass

```python
import math, functools
import jax, jax.numpy as jnp
from jax import lax
import numpy as np

D_MODEL = 1024
BATCH = 1
SEQ = 1024
DEPTH = 1
DEC_BATCH = 8
DEC_SEQ = 1
PAST_LEN = 512
PAGE_SIZE = 128

N_HEADS = 8
HEAD_DIM = 64
D_ATTN = N_HEADS * HEAD_DIM
D_CONV = D_MODEL - D_ATTN
N_IDX_HEADS = 8
IDX_DIM = 64
TOPK_MAX = 256
CONV_WIDTH = 31
FFN_CONV_WIDTH = 3
D_FF = 2816
N_MEM = 256
MEM_HEADS = 4
MEM_HEAD_DIM = 64
D_MEM_ATTN = MEM_HEADS * MEM_HEAD_DIM
REL_BUCKETS = 32
REL_MAX_DIST = 128
Q_BLOCK = 128
D_IN = 3 * D_ATTN + N_IDX_HEADS * IDX_DIM + IDX_DIM + N_IDX_HEADS + 2 * D_CONV
RMS_EPS = 1e-6
LN_EPS = 1e-5
NEG_INF = -1e30

kernel_name = "hymba_dsa_conformer_convffn_decode_step"

def _in_proj_offsets():
    sizes = (D_ATTN, D_ATTN, D_ATTN, N_IDX_HEADS * IDX_DIM, IDX_DIM, N_IDX_HEADS, 2 * D_CONV)
    offs, acc = [], 0
    for s in sizes[:-1]:
        acc += s
        offs.append(acc)
    return offs

def rmsnorm(x, g):
    xf = x.astype(jnp.float32)
    y = xf * lax.rsqrt(jnp.mean(xf * xf, -1, keepdims=True) + RMS_EPS)
    return (y * g.astype(jnp.float32)).astype(x.dtype)

def layernorm(x, g, b):
    xf = x.astype(jnp.float32)
    mu = jnp.mean(xf, -1, keepdims=True)
    var = jnp.mean(jnp.square(xf - mu), -1, keepdims=True)
    y = (xf - mu) * lax.rsqrt(var + LN_EPS)
    return (y * g.astype(jnp.float32) + b.astype(jnp.float32)).astype(x.dtype)

def rel_bucket(rel):
    n = jnp.maximum(rel, 0)
    max_exact = REL_BUCKETS // 2
    nf = jnp.maximum(n, 1).astype(jnp.float32)
    large = max_exact + (jnp.log(nf / max_exact) / math.log(REL_MAX_DIST / max_exact)
                         * (REL_BUCKETS - max_exact)).astype(jnp.int32)
    large = jnp.minimum(large, REL_BUCKETS - 1)
    return jnp.where(n < max_exact, n, large)

def causal_dwconv(x_ext, w, b):
    c = x_ext.shape[-1]
    y = lax.conv_general_dilated(x_ext, w[:, None, :].astype(x_ext.dtype), window_strides=(1,),
                                 padding='VALID', dimension_numbers=('NWC', 'WIO', 'NWC'),
                                 feature_group_count=c)
    return y + b

def indexer_scores(q_idx, w_idx, k_idx):
    s = jnp.einsum('bthd,bsd->bths', q_idx, k_idx) * (IDX_DIM ** -0.5)
    return jnp.einsum('bths,bth->bts', jax.nn.relu(s), w_idx * (N_IDX_HEADS ** -0.5))

def sparse_attend(q, kg, vg, q_pos, key_pos, rel_table):
    rel = q_pos[None, :, None] - key_pos
    bias = jnp.swapaxes(rel_table[rel_bucket(rel)], -1, -2)
    logits = (jnp.einsum('bthd,btkhd->bthk', q, kg).astype(jnp.float32) * (HEAD_DIM ** -0.5)
              + bias.astype(jnp.float32))
    logits = jnp.where((rel >= 0)[:, :, None, :], logits, NEG_INF)
    p = jax.nn.softmax(logits, axis=-1).astype(vg.dtype)
    return jnp.einsum('bthk,btkhd->bthd', p, vg)

def dsa_prompt(rel_table, q, k, v, q_idx, k_idx, w_idx):
    b, s, h, dh = q.shape
    topk = min(TOPK_MAX, s // 4)
    nb = s // Q_BLOCK
    key_pos = jnp.arange(s)
    bidx = jnp.arange(b)[:, None, None]

    def blockify(a):
        return jnp.moveaxis(a.reshape((b, nb, Q_BLOCK) + a.shape[2:]), 1, 0)

    def one_block(args):
        blk, qb, qib, wb = args
        q_pos = blk * Q_BLOCK + jnp.arange(Q_BLOCK)
        sc = indexer_scores(qib, wb, k_idx)
        sc = jnp.where(key_pos[None, None, :] <= q_pos[None, :, None], sc, -jnp.inf)
        _, idx = lax.top_k(sc, topk)
        return sparse_attend(qb, k[bidx, idx], v[bidx, idx], q_pos, idx, rel_table)

    out = lax.map(one_block, (jnp.arange(nb), blockify(q), blockify(q_idx), blockify(w_idx)))
    return jnp.moveaxis(out, 0, 1).reshape(b, s, h * dh)

def dsa_sample(cache_k, cache_v, cache_idx_k, page_table, rel_table, q, k, v, q_idx, k_idx, w_idx):
    db, t, h, dh = q.shape
    n_pages = page_table.shape[1]
    ps = cache_k.shape[1]
    past = n_pages * ps
    l_keys = past + t
    topk = min(TOPK_MAX, l_keys // 4)
    k_idx_past = cache_idx_k[page_table].reshape(db, past, IDX_DIM)
    k_idx_all = jnp.concatenate([k_idx_past.astype(k_idx.dtype), k_idx], axis=1)
    q_pos = past + jnp.arange(t)
    sc = indexer_scores(q_idx, w_idx, k_idx_all)
    sc = jnp.where(jnp.arange(l_keys)[None, None, :] <= q_pos[None, :, None], sc, -jnp.inf)
    _, idx = lax.top_k(sc, topk)
    bidx = jnp.arange(db)[:, None, None]
    pidx = jnp.minimum(idx, past - 1)
    phys = page_table[bidx, pidx // ps]
    off = pidx % ps
    nidx = jnp.clip(idx - past, 0, t - 1)
    sel = (idx < past)[..., None, None]
    kg = jnp.where(sel, cache_k[phys, off].astype(k.dtype), k[bidx, nidx])
    vg = jnp.where(sel, cache_v[phys, off].astype(v.dtype), v[bidx, nidx])
    return sparse_attend(q, kg, vg, q_pos, idx, rel_table).reshape(db, t, h * dh)

def mem_kv(mem, g_mem, w_ckv):
    b, n, _ = mem.shape
    km, vm = jnp.split(rmsnorm(mem, g_mem) @ w_ckv, 2, axis=-1)
    return km.reshape(b, n, MEM_HEADS, MEM_HEAD_DIM), vm.reshape(b, n, MEM_HEADS, MEM_HEAD_DIM)

def mem_attend(h, w_cq, km, vm, w_co):
    b, t, _ = h.shape
    q = (h @ w_cq).reshape(b, t, MEM_HEADS, MEM_HEAD_DIM)
    logits = jnp.einsum('bthd,bnhd->bhtn', q, km.astype(q.dtype)).astype(jnp.float32) * (MEM_HEAD_DIM ** -0.5)
    p = jax.nn.softmax(logits, axis=-1).astype(q.dtype)
    o = jnp.einsum('bhtn,bnhd->bthd', p, vm.astype(q.dtype)).reshape(b, t, D_MEM_ATTN)
    return o @ w_co

def _layer(x, attn_fn, conv_prev, ffn_prev, mem_k, mem_v, lw):
    b, t, _ = x.shape
    h = rmsnorm(x, lw['norm_mix'])
    q, k, v, qi, ki, wi, glu = jnp.split(h @ lw['w_in'], _in_proj_offsets(), axis=-1)
    q = q.reshape(b, t, N_HEADS, HEAD_DIM)
    k = k.reshape(b, t, N_HEADS, HEAD_DIM)
    v = v.reshape(b, t, N_HEADS, HEAD_DIM)
    qi = qi.reshape(b, t, N_IDX_HEADS, IDX_DIM)
    a = attn_fn(q, k, v, qi, ki, wi)
    u = glu[..., :D_CONV] * jax.nn.sigmoid(glu[..., D_CONV:])
    u_ext = jnp.concatenate([conv_prev.astype(u.dtype), u], axis=1)
    c = jax.nn.silu(layernorm(causal_dwconv(u_ext, lw['conv_dw'], lw['conv_db']),
                              lw['conv_ln_g'], lw['conv_ln_b']))
    x = x + jnp.concatenate([a, c], axis=-1) @ lw['w_o']
    x = x + mem_attend(rmsnorm(x, lw['norm_mem_q']), lw['w_cq'], mem_k, mem_v, lw['w_co'])
    up = rmsnorm(x, lw['norm_ffn']) @ lw['w_up']
    up_ext = jnp.concatenate([ffn_prev.astype(up.dtype), up], axis=1)
    g, val = jnp.split(causal_dwconv(up_ext, lw['ffn_dw'], lw['ffn_db']), 2, axis=-1)
    x = x + (jax.nn.silu(g) * val) @ lw['w_down']
    return x, k, v, ki, u_ext[:, -(CONV_WIDTH - 1):], up_ext[:, -(FFN_CONV_WIDTH - 1):]

def setup_inputs(seed: int = 0) -> dict:
    key = jax.random.key(seed)
    ks = jax.random.split(key, 32)
    f32 = jnp.float32

    def nrm(k, shape, scale):
        return jax.random.normal(k, shape, f32) * scale

    n_pages = PAST_LEN // PAGE_SIZE
    n_used = DEC_BATCH * n_pages
    n_pool = (5 * n_used + 3) // 4
    page_table = jax.random.permutation(ks[0], n_pool)[:n_used].reshape(DEC_BATCH, n_pages).astype(jnp.int32)
    return {
        'x_prompt': nrm(ks[1], (BATCH, SEQ, D_MODEL), 1.0),
        'x_sample': nrm(ks[2], (DEC_BATCH, DEC_SEQ, D_MODEL), 1.0),
        'mem_prompt': nrm(ks[3], (BATCH, N_MEM, D_MODEL), 1.0),
        'cache_k': nrm(ks[4], (DEPTH, n_pool, PAGE_SIZE, N_HEADS, HEAD_DIM), 1.0),
        'cache_v': nrm(ks[5], (DEPTH, n_pool, PAGE_SIZE, N_HEADS, HEAD_DIM), 1.0),
        'cache_idx_k': nrm(ks[6], (DEPTH, n_pool, PAGE_SIZE, IDX_DIM), 1.0),
        'page_table': page_table,
        'cache_conv': nrm(ks[7], (DEPTH, DEC_BATCH, CONV_WIDTH - 1, D_CONV), 0.5),
        'cache_ffn': nrm(ks[8], (DEPTH, DEC_BATCH, FFN_CONV_WIDTH - 1, 2 * D_FF), 1.0),
        'cache_mem_k': nrm(ks[9], (DEPTH, DEC_BATCH, N_MEM, MEM_HEADS, MEM_HEAD_DIM), 1.0),
        'cache_mem_v': nrm(ks[10], (DEPTH, DEC_BATCH, N_MEM, MEM_HEADS, MEM_HEAD_DIM), 1.0),
        'rel_bias': nrm(ks[11], (REL_BUCKETS, N_HEADS), 0.5),
        'norm_mix': 1.0 + nrm(ks[12], (DEPTH, D_MODEL), 0.02),
        'w_in': nrm(ks[13], (DEPTH, D_MODEL, D_IN), D_MODEL ** -0.5),
        'conv_dw': nrm(ks[14], (DEPTH, CONV_WIDTH, D_CONV), CONV_WIDTH ** -0.5),
        'conv_db': nrm(ks[15], (DEPTH, D_CONV), 0.02),
        'conv_ln_g': 1.0 + nrm(ks[16], (DEPTH, D_CONV), 0.02),
        'conv_ln_b': nrm(ks[17], (DEPTH, D_CONV), 0.02),
        'w_o': nrm(ks[18], (DEPTH, D_MODEL, D_MODEL), D_MODEL ** -0.5),
        'norm_mem_q': 1.0 + nrm(ks[19], (DEPTH, D_MODEL), 0.02),
        'norm_mem_kv': 1.0 + nrm(ks[20], (DEPTH, D_MODEL), 0.02),
        'w_cq': nrm(ks[21], (DEPTH, D_MODEL, D_MEM_ATTN), D_MODEL ** -0.5),
        'w_ckv': nrm(ks[22], (DEPTH, D_MODEL, 2 * D_MEM_ATTN), D_MODEL ** -0.5),
        'w_co': nrm(ks[23], (DEPTH, D_MEM_ATTN, D_MODEL), D_MEM_ATTN ** -0.5),
        'norm_ffn': 1.0 + nrm(ks[24], (DEPTH, D_MODEL), 0.02),
        'w_up': nrm(ks[25], (DEPTH, D_MODEL, 2 * D_FF), D_MODEL ** -0.5),
        'ffn_dw': nrm(ks[26], (DEPTH, FFN_CONV_WIDTH, 2 * D_FF), FFN_CONV_WIDTH ** -0.5),
        'ffn_db': nrm(ks[27], (DEPTH, 2 * D_FF), 0.02),
        'w_down': nrm(ks[28], (DEPTH, D_FF, D_MODEL), D_FF ** -0.5),
        'norm_final': 1.0 + nrm(ks[29], (D_MODEL,), 0.02),
    }

def reference(x_prompt, x_sample, mem_prompt, cache_k, cache_v, cache_idx_k, page_table, cache_conv,
              cache_ffn, cache_mem_k, cache_mem_v, rel_bias, norm_mix, w_in, conv_dw, conv_db, conv_ln_g,
              conv_ln_b, w_o, norm_mem_q, norm_mem_kv, w_cq, w_ckv, w_co, norm_ffn, w_up, ffn_dw, ffn_db,
              w_down, norm_final):
    yp, ys = x_prompt, x_sample
    bp = x_prompt.shape[0]
    kp_l, vp_l, kip_l, cp_l, fp_l, mkp_l, mvp_l = [], [], [], [], [], [], []
    ks_l, vs_l, kis_l, cs_l, fs_l = [], [], [], [], []
    for l in range(DEPTH):
        lw = dict(norm_mix=norm_mix[l], w_in=w_in[l], conv_dw=conv_dw[l], conv_db=conv_db[l],
                  conv_ln_g=conv_ln_g[l], conv_ln_b=conv_ln_b[l], w_o=w_o[l], norm_mem_q=norm_mem_q[l],
                  w_cq=w_cq[l], w_co=w_co[l], norm_ffn=norm_ffn[l], w_up=w_up[l], ffn_dw=ffn_dw[l],
                  ffn_db=ffn_db[l], w_down=w_down[l])
        mkp, mvp = mem_kv(mem_prompt, norm_mem_kv[l], w_ckv[l])
        conv0 = jnp.zeros((bp, CONV_WIDTH - 1, D_CONV), yp.dtype)
        ffn0 = jnp.zeros((bp, FFN_CONV_WIDTH - 1, 2 * D_FF), yp.dtype)
        yp, kp, vp, kip, cp, fp = _layer(yp, functools.partial(dsa_prompt, rel_bias), conv0, ffn0,
                                         mkp, mvp, lw)
        attn_s = functools.partial(dsa_sample, cache_k[l], cache_v[l], cache_idx_k[l], page_table, rel_bias)
        ys, k_s, v_s, ki_s, c_s, f_s = _layer(ys, attn_s, cache_conv[l], cache_ffn[l],
                                             cache_mem_k[l], cache_mem_v[l], lw)
        kp_l.append(kp); vp_l.append(vp); kip_l.append(kip); cp_l.append(cp); fp_l.append(fp)
        mkp_l.append(mkp); mvp_l.append(mvp)
        ks_l.append(k_s); vs_l.append(v_s); kis_l.append(ki_s); cs_l.append(c_s); fs_l.append(f_s)
    y_prompt = rmsnorm(yp, norm_final)
    y_sample = rmsnorm(ys, norm_final)
    k_prompt = jnp.stack(kp_l); v_prompt = jnp.stack(vp_l); idx_k_prompt = jnp.stack(kip_l)
    k_sample = jnp.stack(ks_l); v_sample = jnp.stack(vs_l); idx_k_sample = jnp.stack(kis_l)
    conv_prompt = jnp.stack(cp_l); conv_sample = jnp.stack(cs_l)
    ffn_prompt = jnp.stack(fp_l); ffn_sample = jnp.stack(fs_l)
    mem_k_prompt = jnp.stack(mkp_l); mem_v_prompt = jnp.stack(mvp_l)
    return (y_prompt, y_sample, k_prompt, v_prompt, idx_k_prompt, k_sample, v_sample, idx_k_sample,
            conv_prompt, conv_sample, ffn_prompt, ffn_sample, mem_k_prompt, mem_v_prompt)


_drawn_inputs = setup_inputs


def setup_inputs(seed=0):
    import zlib

    import numpy as np

    out = dict(_drawn_inputs(seed))
    spreads = {}
    factors = {'norm_mix': 2.754,
     'conv_db': 3.374,
     'conv_ln_g': 5.468,
     'conv_ln_b': 6.411,
     'norm_mem_q': 8.0,
     'norm_mem_kv': 2.938,
     'norm_ffn': 2.913,
     'ffn_db': 4.049,
     'norm_final': 2.883}
    for name, (base, spread) in spreads.items():
        noise = np.random.default_rng([zlib.crc32(name.encode()), seed]).standard_normal(out[name].shape)
        drawn = base * np.exp(spread * noise) if base else spread * noise
        out[name] = __import__('jax').numpy.asarray(drawn.astype(out[name].dtype))
    for name, factor in factors.items():
        out[name] = (out[name] * factor).astype(out[name].dtype)
    return out
```

```python
from contextlib import ExitStack

import numpy as np

import concourse.bass as bass
from concourse import mybir

F32 = mybir.dt.float32
F32R = mybir.dt.float32r
I32 = mybir.dt.int32
ALU = mybir.AluOpType
ACT = mybir.ActivationFunctionType
AX = mybir.AxisListType

P = 128
D = 1024
KT = D // P
S = 1024
NB = S // P
DB = 8
T = S + DB
CH = T // 3
NH = 8
DH = 64
DA = NH * DH
CT = DA // P
PAST = 512
NPG = PAST // P
TOPK = 256
TOPK_S = (PAST + 1) // 4
CW = 31
HALO = CW - 1
NM = 256
MH = 4
DFF = 2816
FT = DFF // P
NG = FT // 2
REPLACED = -3.4e38
CAUSAL = -3.0e38
NEG = -1e30
TAKEN = -3.35e38
NIN = 25
RMS_EPS, LN_EPS = 1e-6, 1e-5
R8 = 8 ** -0.5


def bucket(n):
    n = max(n, 0)
    if n < 16:
        return n
    return min(16 + int(np.float32(np.log(np.float32(n) / 16) / np.log(8.0) * 16)), 31)


def constants():
    toep = np.zeros((32, 384), np.float32)
    for i in range(384):
        toep[bucket(255 - i), i] += 8.0
        toep[31, i] -= 8.0
    samp = np.zeros((32, PAST + 1), np.float32)
    for k in range(PAST + 1):
        samp[bucket(PAST - k), k] = 8.0
    causal = np.where(np.arange(P)[None, :] <= np.arange(P)[:, None], 0.0, NEG).astype(np.float32)
    same = (np.arange(64)[:, None] // 8 == np.arange(8)[None, :]).astype(np.float32)
    return {
        "c_ident": np.eye(P, dtype=np.float32), "c_toep": toep, "c_samp": samp, "c_causal": causal,
        "c_same": same, "c_sameT": np.ascontiguousarray(same.T),
    }


class Chain:

    def __init__(self, eng, sem):
        self.eng, self.sem, self.n = eng, sem, 0

    def link(self, ins):
        ins.then_inc(self.sem, 1)
        self.n = self.n + 1
        self.eng.wait_ge(self.sem, self.n)



def order_of_w_in():
    steps = [("slot", j) for j in range(5)] + [("ki", 0)]
    idx = [("idx", b) for b in range(2, NB)]
    for m in range(4):
        steps += [("slot", 5 + m), ("ktok", m)] + idx[:2]
        idx = idx[2:]
    for m in range(4):
        steps += [("slot", 9 + m), ("vtok", m)]
    steps += [("slot", 13 + m) for m in range(4)]
    steps += [("slot", 17 + m) for m in range(8)] + [("ctok", 0)]
    return steps


def aux_before(what, i=0):
    n = 0
    for kind, j in order_of_w_in():
        if (kind, j) == (what, i):
            return n
        n += {"slot": 0, "ki": 3, "ktok": 3, "vtok": 3, "ctok": 4}.get(kind, 8 * (1 + (j > 3)))
    return n


IN_SLOTS = ([("qi", m, 1536 + m * P, P) for m in range(4)] + [("kw", 0, 2048, 72)]
            + [("k", m, 512 + m * P, P) for m in range(4)] + [("v", m, 1024 + m * P, P) for m in range(4)]
            + [("q", m, m * P, P) for m in range(4)]
            + [x for m in range(4) for x in (("ga", m, 2120 + m * P, P), ("gb", m, 2632 + m * P, P))])
SLOT_CKV, SLOT_IN = 0, 4
SLOT_O = SLOT_IN + NIN
SLOT_CQ = SLOT_O + 8
SLOT_CO = SLOT_CQ + 2
SLOT_F = SLOT_CO + 2
SLOTS = SLOT_F + 6 * NG


def ffn_slot(r):
    if r < 4:
        return "up", 0, r
    if r >= 6 * NG - 2:
        return "down", NG - 1, r - (6 * NG - 2)
    g, q = divmod(r - 4, 6)
    return ("up", g + 1, q) if q < 4 else ("down", g, q - 4)


def up_tile(g, q):
    return 2 * g + q // 2 + (q % 2) * FT


def units_of(j):
    if j < SLOT_IN:
        return 1
    if j < SLOT_CO:
        return 3
    if j < SLOT_F:
        return 12
    r = j - SLOT_F
    if r < 4:
        return 3
    return 12 if r >= 6 * NG - 2 or (r - 4) % 6 >= 4 else 3


UNITS_TO = [sum(units_of(i) for i in range(j)) for j in range(SLOTS + 1)]
FFN0 = UNITS_TO[SLOT_F]
DOWN_END = [UNITS_TO[SLOT_F + r + 1] for r in range(6 * NG) if ffn_slot(r)[0] == "down" and ffn_slot(r)[2] == 1]
RES_AT = {1: 6, 2: 6 + 24, 3: 6 + 48 + 24 * NG - 24}
IDX_EXT = {b: P * (b + 1) for b in range(2, NB)}
IDX_AT = {b: sum(IDX_EXT[i] for i in range(2, b)) for b in range(2, NB)}
IDX_UNITS = [(b, h, f, min(512, IDX_EXT[b] - 512 * f)) for b in range(2, NB) for h in range(NH)
             for f in range(-(-IDX_EXT[b] // 512))]
IDX_AUX = [aux_before("idx", b) + sum(1 for x in IDX_UNITS[:n] if x[0] == b) + 1 for n, (b, _, _, _) in enumerate(IDX_UNITS)]
AUX_IN = aux_before("end")
ITEMS = [(b, h) for b in range(NB) for h in range(NH)]
N_ITEMS, N_LATE, N_PAGES = len(ITEMS), sum(1 for b, _ in ITEMS if b >= 4), DB * NPG


def build(nc, a, o):
    ctx = ExitStack()
    base = (nc.sbuf_base + 63) // 64 * 64

    class Region:

        def __init__(self, start, size):
            self.start, self.end, self.at = start, start + size, start

        def take(self, name, shape, dt=F32):
            n = int(np.prod(shape[1:])) * 4
            t = nc.alloc_sbuf_tensor_at(name, shape, dt, offset=self.at)
            self.at += (n + 31) // 32 * 32
            assert self.at <= self.end, (name, self.at - self.start, self.end - self.start)
            return t

        def again(self, skip=0):
            return Region(self.start + skip, self.end - self.start - skip)

    XB = KT * T * 4
    rc = Region(base, 14496)
    rw = Region(rc.end, 6 * 4096)
    rh = Region(rw.end, 2 * XB)
    rx = Region(rh.end, XB)
    rz = Region(rx.end, nc.sbuf_usable_end - rx.end)
    rxz = Region(rx.start, rz.end - rx.start)

    def sem(name):
        return ctx.enter_context(nc.semaphore(name))

    ident = rc.take("ident", [P, P])
    ones = rc.take("ones", [P, P])
    causal = rc.take("causal", [P, P])
    same = rc.take("same", [64, 8])
    sameT = rc.take("sameT", [8, 64])
    ptab = rc.take("ptab", [1, DB * NPG], I32)
    vec = rc.take("vec", [P, 52])
    cw = rc.take("cw", [P, CW * CT])
    fw = rc.take("fw", [P, 4, 2 * FT])
    cf = rc.take("cf", [P, DB, 2, 2 * FT])
    wj = rc.take("wj", [P, 9, 8])
    s8 = rc.take("s8", [P, 8])
    usr = rc.take("usr", [P, CT, 8])
    kmT = rc.take("kmT", [P, 2, NM])
    vm = rc.take("vm", [P, 2, NM])
    wr = [rw.take(f"w_raw{i}", [P, KT * P]) for i in range(2)]
    wh = [rw.take(f"w_hi{i}", [P, KT * P], F32R) for i in range(2)]
    wl = [rw.take(f"w_lo{i}", [P, KT * P], F32R) for i in range(2)]
    hh = rh.take("h_hi", [P, KT, T], F32R)
    hl = rh.take("h_lo", [P, KT, T], F32R)
    xT = rx.take("xT", [P, KT, T])
    ps = ctx.enter_context(nc.psum_tensor("ps", [P, 8, 512], F32))

    r = rh.again()
    xs = r.take("x_tok", [P, NB, D])
    xsm = r.take("x_sam", [DB, D])
    r = rz.again()
    mtok = r.take("mem_tok", [P, 2, D])
    memT = r.take("memT", [P, KT, NM])
    mhh = r.take("mem_hi", [P, KT, NM], F32R)
    r2 = r.again(r.at - r.start)
    mvT = r2.take("mem_vT", [P, 2, NM])
    mtk = r2.take("mem_kv_tok", [P, 2, 2 * NM])
    r3 = rz.again(r2.start - rz.start)
    msq = r3.take("mem_sq", [P, KT, NM])
    mhl = r3.take("mem_lo", [P, KT, NM], F32R)
    r3 = rz.again(r3.at - rz.start)
    mr = r3.take("mem_r", [P, NM])
    norm_at = (rz.end - rz.start - 5 * (4 * T)) // 32 * 32
    rn = rz.again(norm_at)
    nsq = [rn.take(f"n_sq{i}", [P, T]) for i in range(2)]
    nr = rn.take("n_rstd", [P, T])
    nh_ = [rn.take(f"n_h{i}", [P, T]) for i in range(2)]
    rn = r3.again(r3.at - r3.start)
    prm = rn.take("prm", [52, P])
    cwr = rn.take("cwr", [CW * CT, P])
    fwr = rn.take("fwr", [2 * FT, 4, P])
    cfr = rn.take("cfr", [2 * 2 * FT, DB, P])
    rbt = rn.take("rbt", [32, NH])
    toep = rn.take("toep", [32, 384])
    tst = rn.take("tst", [P, NH, 384])
    rbx = rn.take("rbx", [32, NH, P])

    r = rxz.again()
    qx = r.take("qx", [P, CT, T])
    kT_ = r.take("kT", [P, CT, T])
    sc = r.take("sc", [P, sum(IDX_EXT.values())])
    u = r.take("u", [P, CT, HALO + S])
    kw = r.take("kw", [72, T])
    ki2 = r.take("ki2", [P, T])
    us = r.take("us", [P, CT, DB, CW])
    ksm = r.take("ksm", [DB, 2, DA])
    mid = r.at - rxz.start
    ga = r.take("ga", [P, T])
    gb = [r.take(f"gb{i}", [P, CH]) for i in range(2)]
    rr = [r.take(f"rr{i}", [P, 512]) for i in range(2)]
    kit = r.again(r.at - r.start).take("kit", [P, NB, DH])
    vT1 = r.take("vT1", [P, T])
    ks = [r.take(f"ks{i}", [P, NB, P]) for i in range(2)]
    r = rxz.again(mid)
    cpt = r.take("cpt", [HALO, DA])
    cst = r.take("cst", [DB, DA])
    r = rxz.again(mid + 4 * T + 8 * CH)
    ccr = r.take("ccr", [4 * HALO, 2, DA])
    kism = rc.take("kism", [DB, DH])

    rl = rh.again(XB + 4 * T * 4)
    y = rl.take("conv_sum", [P, CT, T])
    r = rxz.again(mid)
    lq = [r.take(f"ln_sq{i}", [P, T]) for i in range(2)]
    lr = r.take("ln_rstd", [P, T])
    lh = [r.take(f"ln_h{i}", [P, T]) for i in range(2)]
    r = rxz.again(mid)
    v_ = r.take("v", [P, NB, DA])
    lg = [r.take(f"logits{i}", [P, S]) for i in range(2)]
    r = rxz.again(2 * CT * 4 * T + 16896)
    bt = r.take("bt", [P, NH, 2 * P])
    nb = r.take("nb", [P, NH, 2 * P])
    r = rxz.again(2 * CT * 4 * T + 16896 + 16864)
    pt = [r.take(f"probsT{i}", [P, NB, P]) for i in range(2)]
    att = r.take("att", [P, DA])
    mx = rc.take("mx", [P, 4, 4])
    rs = rc.take("rs", [P, 2, 8])
    ri = rc.take("ri", [P, 2, 8])
    kws = rc.take("kws", [72, 8])

    KEYS = PAST + 1
    qis = rc.take("qis", [64, DB, NH])
    wsel = rc.take("wsel", [NH, DB, DB])
    r = rxz.again(2 * CT * 4 * T)
    kip = r.take("s_idx_pages", [P, DB * NPG, DH])
    kis = [r.take(f"s_idxT{i}", [DH, PAST]) for i in range(2)]
    rsm = [r.take(f"s_relu{i}", [NH, KEYS]) for i in range(2)]
    ssc = r.take("s_scores", [DB, KEYS])
    adds = r.take("s_adds", [64, KEYS])
    ls = r.take("s_logits", [64, KEYS])
    kpt = [r.take(f"s_kT{i}", [P, CT, P]) for i in range(2)]
    qbd = r.take("s_q_heads", [P, CT, DB, NH])
    sl = r.take("s_logitsT", [P, NPG, 64])
    spT = r.take("s_probsT", [P, NPG, 64])
    pd = r.take("s_self_prob", [64, 8])
    pdT = r.take("s_self_probT", [8, 64])
    srb = r.take("s_rel", [32, DB, NH])
    srb1 = r.take("s_rel1", [32, NH])
    samp = r.take("s_onehot", [32, KEYS])
    ssm = r.take("s_small", [64, 8])
    sself = r.take("s_self", [64, 8])
    aself = r.take("s_att", [P, CT, DB])
    assert r.at <= rxz.start + mid - 4096
    r = rxz.again(mid)
    kpg = [r.take(f"s_k_page{i}", [P, DA]) for i in range(4)]
    vpg = [r.take(f"s_v_pages{i}", [P, NPG, DA]) for i in range(2)]

    r = rz.again()
    qc = r.take("qc", [P, 2, T])
    xp = [r.take(f"x_probs{i}", [P, MH, NM]) for i in range(2)]
    xpt = [r.take(f"x_probsT{i}", [P, 2 * MH, P]) for i in range(2)]
    xa = r.take("x_att", [P, MH * DH])
    xh = r.take("x_hi", [P, 2, T], F32R)
    xl = r.take("x_lo", [P, 2, T], F32R)
    xkp = [r.take(f"x_k{i}", [P, 2, NM]) for i in range(2)]
    xvp = [r.take(f"x_v{i}", [P, 2, NM]) for i in range(2)]
    xkt = [r.take(f"x_kT{i}", [P, 2, 2, P]) for i in range(2)]
    xqb = r.take("x_q_heads", [P, 2, DB, MH])
    xsl = r.take("x_logitsT", [P, 2, DB * MH])
    xls = r.take("x_logits", [DB * MH, NM])
    xsp = r.take("x_sprobsT", [P, 2, DB * MH])
    xss = r.take("x_small", [DB * MH, 4])
    xas = r.take("x_satt", [P, 2, DB])
    xm = rc.take("xm", [P, 2, 3, MH])
    r = rz.again()
    upl = r.take("upl", [P, 10, 2 * FT])
    out_at = r.at - rz.start
    ue = [r.take(f"up{i}", [P, 2 + T]) for i in range(2)]
    uy = [r.take(f"up_conv{i}", [P, T]) for i in range(4)]
    gh = [r.take(f"g_hi{i}", [P, 2, T], F32R) for i in range(2)]
    gl = [r.take(f"g_lo{i}", [P, 2, T], F32R) for i in range(2)]
    r = rz.again(out_at)
    fst = r.take("ffn_out", [2 * 2 * FT, 5, P])
    ytk = [r.take(f"y_tok{i}", [P, D]) for i in range(2)]
    yT = rh.again().take("yT", [P, KT, T])

    x_spill = nc.dram_tensor("x_spill", [P, KT * T], F32).ap()
    toep_d = nc.dram_tensor("toep_d", [P, NH * 384], F32).ap()

    par_in, x_in, mem_in = sem("par_in"), sem("x_in"), sem("mem_in")
    ones_ok = sem("ones_ok")
    par_t, par_c = sem("par_t"), sem("par_c")
    toep_out, rbx_ok, tp_t, tp_c = sem("toep_out"), sem("rbx_ok"), sem("tp_t"), sem("tp_c")
    xt_t, xt_c = sem("xt_t"), sem("xt_c")
    w_hi, w_lo, g_done = sem("w_hi"), sem("w_lo"), sem("g_done")
    w_raw = [sem(f"w_raw{i}_in") for i in range(2)]
    n_sq, n_acc, n_ss, n_var, n_rstd = sem("n_sq"), sem("n_acc"), sem("n_ss"), sem("n_var"), sem("n_rstd")
    n_h, n_hi, n_lo = sem("n_h"), sem("n_hi"), sem("n_lo")
    spilled = sem("spilled")
    dve_self, act_self, pool_self = sem("dve_self"), sem("act_self"), sem("pool_self")
    mt_t, mt_c = sem("mt_t"), sem("mt_c")
    m_sq, m_ss, m_var, m_rstd, m_h, m_hi, m_lo = (sem("m_" + x) for x in ("sq", "ss", "var", "rstd", "h", "hi", "lo"))
    ckv_c, mkv_t, mkv_c = sem("ckv_c"), sem("mkv_t"), sem("mkv_c")
    mem_out = sem("mem_out")
    NPAR = 19
    in_c, aux_t, aux_c, ki_dup, ki_out = sem("in_c"), sem("aux_t"), sem("aux_c"), sem("ki_dup"), sem("ki_out")
    idx_c, gb_ok, u_ok = sem("idx_c"), sem("gb_ok"), sem("u_ok")
    kv_out = [sem(f"kv_out{i}") for i in range(2)]
    ksm_out, cc_in, conv_out = sem("ksm_out"), sem("cc_in"), sem("conv_out")
    tap, y_ok, ln_s, ln_c, ln_sq, ln_ss = (sem(x) for x in ("tap", "y_ok", "ln_s", "ln_c", "ln_sq", "ln_ss"))
    ln_var, ln_rstd, ln_h, ln_act, ln_hi, ln_lo = (sem(x) for x in ("ln_var", "ln_rstd", "ln_h", "ln_act", "ln_hi", "ln_lo"))
    bt_in, v_in, bt_ok, nb_ok = sem("bt_in"), sem("v_in"), sem("bt_ok"), sem("nb_ok")
    qk, added, mx_ok, exp_ok = sem("qk"), sem("added"), sem("mx_ok"), sem("exp_ok")
    t0_t, t1_t, t0_c, t1_c, pv = sem("t0_t"), sem("t1_t"), sem("t0_c"), sem("t1_c"), sem("pv")
    att_ok, aT_t, aT_hi, aT_lo = sem("att_ok"), sem("aT_t"), sem("aT_hi"), sem("aT_lo")

    A = a
    block = ctx.enter_context(nc.Block())

    kip_in, srb_in, srb_ok, qbd_ok = sem("kip_in"), sem("srb_in"), sem("srb_ok"), sem("qbd_ok")
    kp_in = [sem(f"kp_in{i}") for i in range(4)]
    vp_in = [sem(f"vp_in{i}") for i in range(2)]
    wsel_ok, qbd_z = sem("wsel_ok"), sem("qbd_z")
    si_t, si_c, si_s, si_r, si_w = (sem("si_" + x) for x in "tcsrw")
    smask, sk_t, sk_c, sk_s, sl_c, sl_t, sb_t, sb_c = (sem(x) for x in ("smask", "sk_t", "sk_c", "sk_s", "sl_c", "sl_t", "sb_t", "sb_c"))
    s_nm, s_exp, s_p, sp_t, sp_c, sv_t, s_att, s_hi, s_lo = (sem(x) for x in ("s_nm", "s_exp", "s_p", "sp_t", "sp_c", "sv_t", "s_att", "s_hi", "s_lo"))

    x_back, res_c, qc_c = sem("x_back"), sem("res_c"), sem("qc_c")
    xk_in = [sem(f"xk_in{i}") for i in range(2)]
    xv_in = [sem(f"xv_in{i}") for i in range(2)]
    f_c, cv, slu, prd, ghi, glo = (sem(x) for x in ("f_c", "cv", "slu", "prd", "ghi", "glo"))
    fo_t, fo_c, ffn_out, yo_t, yo_a, yo_d = (sem(x) for x in ("fo_t", "fo_c", "ffn_out_sem", "yo_t", "yo_a", "yo_d"))
    y_out = [sem(f"y_out{i}") for i in range(2)]

    def pair(n):
        return ps[:, 2 * (n % 2):2 * (n % 2) + 2, :].rearrange("p a n -> p (a n)")

    def late(n):
        return sum(1 for b, _ in ITEMS[:n] if b >= 4)

    def slot_source(j):
        raw = wr[j % 2]
        tile8 = raw[:, :].rearrange("p (k n) -> p k n", n=P)
        tile2 = raw[:, :].rearrange("p (k n) -> p k n", n=512)
        rows = lambda w: w[0].rearrange("(k p) n -> p k n", p=P)
        if j < SLOT_IN:
            return rows(A["w_ckv"])[:, :, j * P:(j + 1) * P], tile8
        if j < SLOT_O:
            _, _, c0, n = IN_SLOTS[j - SLOT_IN]
            return rows(A["w_in"])[:, :, c0:c0 + n], tile8[:, :, 0:n]
        if j < SLOT_CQ:
            m = j - SLOT_O
            return rows(A["w_o"])[:, :, m * P:(m + 1) * P], tile8
        if j < SLOT_CO:
            m = j - SLOT_CQ
            return rows(A["w_cq"])[:, :, m * P:(m + 1) * P], tile8
        if j >= SLOT_F:
            kind, g, q = ffn_slot(j - SLOT_F)
            if kind == "up":
                m = up_tile(g, q)
                return rows(A["w_up"])[:, :, m * P:(m + 1) * P], tile8
            down = A["w_down"][0, 2 * P * g:2 * P * (g + 1), :].rearrange("(k p) n -> p k n", p=P)
            return down[:, :, q * 512:(q + 1) * 512], tile2
        m = j - SLOT_CO
        return rows(A["w_co"])[:, :, m * 512:(m + 1) * 512], tile2

    def w8(w, j):
        return w[j % 2][:, :].rearrange("p (k n) -> p k n", n=P)

    @block.sync
    def _(sp):
        sp.dma_start(xs[:, 0:4, :], A["x_prompt"][0, 0:512, :].rearrange("(t p) d -> p t d", p=P)).then_inc(x_in, 16)
        for t, src in ((ident, "c_ident"), (causal, "c_causal"), (same, "c_same"), (sameT, "c_sameT"),
                       (rbt, "rel_bias"), (toep, "c_toep")):
            sp.dma_start(t[:, :], A[src]).then_inc(par_in, 16)
        for i, n in enumerate(("norm_mix", "norm_mem_q", "norm_mem_kv", "norm_ffn")):
            sp.dma_start(prm[8 * i:8 * i + 8, :], A[n][0].rearrange("(r c) -> r c", c=P)).then_inc(par_in, 16)
        sp.dma_start(prm[32:40, :], A["norm_final"].rearrange("(r c) -> r c", c=P)).then_inc(par_in, 16)
        for i, n in enumerate(("conv_db", "conv_ln_g", "conv_ln_b")):
            sp.dma_start(prm[40 + 4 * i:44 + 4 * i, :], A[n][0].rearrange("(r c) -> r c", c=P)).then_inc(par_in, 16)
        sp.dma_start(cwr[:, :], A["conv_dw"][0].rearrange("j (c p) -> (j c) p", p=P)).then_inc(par_in, 16)
        sp.dma_start(fwr[:, 0:3, :], A["ffn_dw"][0].rearrange("j (c p) -> c j p", p=P)).then_inc(par_in, 16)
        sp.dma_start(fwr[:, 3, :], A["ffn_db"][0].rearrange("(c p) -> c p", p=P)).then_inc(par_in, 16)
        sp.dma_start(cfr[:, :, :], A["cache_ffn"][0].rearrange("b j (c p) -> (j c) b p", p=P)).then_inc(par_in, 16)
        sp.dma_start(ptab[:, :], A["page_table"].rearrange("b j -> (b j)").unsqueeze(0)).then_inc(par_in, 16)
        sp.dma_start(mtok[:, :, :], A["mem_prompt"][0].rearrange("(t p) d -> p t d", p=P)).then_inc(mem_in, 16)
        sp.dma_start(xs[:, 4:8, :], A["x_prompt"][0, 512:1024, :].rearrange("(t p) d -> p t d", p=P)).then_inc(x_in, 16)
        sp.dma_start(xsm[:, :], A["x_sample"][:, 0, :]).then_inc(x_in, 16)
        sp.wait_ge(xt_c, 2 * NB + 1)
        sp.dma_start(x_spill, xT[:, :, :].rearrange("p k t -> p (k t)")).then_inc(spilled, 16)

        def load(j):
            if j >= 2:
                sp.wait_ge(w_lo, j - 1)
            src, dst = slot_source(j)
            sp.dma_start(dst, src).then_inc(w_raw[j % 2], 16)

        for j in range(SLOT_O):
            load(j)
        sp.wait_ge(idx_c, len(IDX_UNITS))
        sp.dma_start(ccr[:, :, :], A["cache_conv"][0].rearrange("(g b) j c -> (b j) g c", g=2)).then_inc(cc_in, 16)
        sp.dma_start(o["conv_sample"][0, :, 0:HALO - 1, :], A["cache_conv"][0, :, 1:HALO, :]).then_inc(conv_out, 16)
        load(SLOT_O)
        load(SLOT_O + 1)
        sp.wait_ge(ln_lo, CT)
        toeplitz = bass.AP(toep_d.tensor, P - 1, [[NH * 384 - 1, P], [384, NH], [1, 2 * P]])
        sp.dma_start(bt[:, :, :], toeplitz).then_inc(bt_in, 16)
        for r in range(2):
            sp.wait_ge(kv_out[r], 64)
        sp.dma_start(v_[:, :, :], o["v_prompt"][0, 0].rearrange("(t p) h d -> p t (h d)", p=P)).then_inc(v_in, 16)
        sp.wait_ge(aT_lo, NB)
        sp.dma_start(srb1[:, :], A["rel_bias"]).then_inc(srb_in, 16)
        sp.dma_start(samp[:, :], A["c_samp"]).then_inc(srb_in, 16)

        def page(i):
            return sp.value_load(ptab[0:1, i:i + 1], min_val=0, max_val=A["cache_k"].shape[1] - 1)

        for i in range(DB * NPG):
            sp.dma_start(kip[:, i, :], A["cache_idx_k"][0, bass.ds(page(i), 1)].rearrange("a p d -> p (a d)")).then_inc(kip_in, 16)
        for i in range(DB * NPG):
            if i >= 4:
                sp.wait_ge(sk_t, i - 3)
            sp.dma_start(kpg[i % 4][:, :], A["cache_k"][0, bass.ds(page(i), 1)].rearrange("a p h d -> p (a h d)")).then_inc(kp_in[i % 4], 16)
        for b in range(DB):
            if b >= 2:
                sp.wait_ge(sv_t, b - 1)
            for q in range(NPG):
                sp.dma_start(vpg[b % 2][:, q, :], A["cache_v"][0, bass.ds(page(NPG * b + q), 1)].rearrange("a p h d -> p (a h d)")).then_inc(vp_in[b % 2], 16)
        sp.wait_ge(s_lo, 1)
        sp.dma_start(xT[:, :, :].rearrange("p k t -> p (k t)"), x_spill).then_inc(x_back, 16)
        for j in range(SLOT_O + 2, SLOT_CO):
            load(j)
        sp.wait_ge(n_lo, 2 * KT)
        for b in range(DB):
            if b >= 2:
                sp.wait_ge(sk_t, N_PAGES + b - 1)
            sp.dma_start(xkp[b % 2][:, :, :], A["cache_mem_k"][0, b].rearrange("(t p) h d -> p t (h d)", p=P)).then_inc(xk_in[b % 2], 16)
        for b in range(DB):
            if b >= 2:
                sp.wait_ge(sv_t, DB + b - 1)
            sp.dma_start(xvp[b % 2][:, :, :], A["cache_mem_v"][0, b].rearrange("(t p) h d -> p t (h d)", p=P)).then_inc(xv_in[b % 2], 16)
        for j in range(SLOT_CO, SLOTS):
            load(j)
        sp.dma_start(o["ffn_sample"][0, :, 0, :], A["cache_ffn"][0, :, 1, :]).then_inc(ffn_out, 16)
        sp.wait_ge(fo_c, 2)
        sp.dma_start(o["ffn_prompt"][0, 0].rearrange("j (c p) -> (j c) p", p=P), fst[:, 0, :]).then_inc(ffn_out, 16)
        for b in range(DB):
            e = b % 2
            sp.dma_start(o["ffn_sample"][0, b, 1].rearrange("(c p) -> c p", p=P), fst[2 * FT * e:2 * FT * (e + 1), 1 + b // 2, :]).then_inc(ffn_out, 16)
        for t in range(NB + 1):
            sp.wait_ge(yo_a, t + 1)
            sp.wait_ge(yo_d, t + 1)
            if t < NB:
                sp.dma_start(o["y_prompt"][0, t * P:(t + 1) * P, :], ytk[t % 2][:, :]).then_inc(y_out[t % 2], 16)
            else:
                sp.dma_start(o["y_sample"][:, 0, :], ytk[t % 2][0:DB, :]).then_inc(y_out[t % 2], 16)
        sp.wait_ge(y_out[0], 16 * 5)
        sp.wait_ge(y_out[1], 16 * 4)
        sp.wait_ge(ffn_out, 16 * (2 + DB))

    @block.gpsimd
    def _(pool):
        self_ = Chain(pool, pool_self)
        pool.memset(ones[:, :], 1.0).then_inc(ones_ok, 1)
        pool.memset(wsel[:, :, :], 0.0).then_inc(wsel_ok, 1)

        def split(j):
            pool.wait_ge(w_raw[j % 2], 16 * (j // 2 + 1))
            if j >= 2:
                pool.wait_ge(g_done, UNITS_TO[j - 1])
            n = IN_SLOTS[j - SLOT_IN][3] if SLOT_IN <= j < SLOT_O else P
            view = lambda w: w[j % 2][:, :].rearrange("p (k n) -> p k n", n=P)[:, :, 0:n]
            pool.tensor_scalar(view(wh), view(wr), 1.0, 0.0, ALU.mult, ALU.add).then_inc(w_hi, 1)
            pool.wait_ge(w_hi, j + 1)
            pool.tensor_tensor(view(wl), view(wr), view(wh).bitcast(F32), ALU.subtract).then_inc(w_lo, 1)

        for j in range(SLOT_IN):
            split(j)

        def gate(m):
            for c in range(3):
                n = 3 * m + c
                t0, t1 = c * CH, min((c + 1) * CH, S)
                pool.wait_ge(gb_ok, n + 1)
                mm = pool.tensor_tensor(u[:, m, HALO + t0:HALO + t1], ga[:, t0:t1], gb[n % 2][:, 0:t1 - t0], ALU.mult)
                if c == 2:
                    mm = pool.tensor_tensor(us[:, m, :, HALO], ga[:, S:T], gb[n % 2][:, S - t0:CH], ALU.mult)
                mm.then_inc(u_ok, 1)

        for js in range(NIN):
            split(SLOT_IN + js)
            if js == 17:
                pool.memset(u[:, :, 0:HALO], 0.0)
            if js >= 20 and js % 2 == 0:
                gate((js - 20) // 2)
        gate(3)
        split(SLOT_O)
        split(SLOT_O + 1)

        pool.wait_ge(bt_in, 16)
        pool.tensor_tensor(bt[:, :, P:2 * P], bt[:, :, P:2 * P], causal[:, :].unsqueeze(1).to_broadcast([P, NH, P]),
                           ALU.add).then_inc(bt_ok, 1)
        pool.wait_ge(bt_ok, 1)
        for b in range(2, NB):
            if b > 2:
                pool.wait_ge(added, NH * b)
            near = sc[:, IDX_AT[b] + P * (b - 1):IDX_AT[b] + P * (b + 1)]
            pool.tensor_tensor(nb[:, :, :], bt[:, :, :], near.unsqueeze(1).to_broadcast([P, NH, 2 * P]),
                               ALU.add).then_inc(nb_ok, 1)
        pool.wait_ge(aT_lo, NB)
        pool.memset(qbd[:, :, :, :], 0.0).then_inc(qbd_z, 1)
        for j in range(SLOT_O + 2, SLOT_CO):
            split(j)
        pool.wait_ge(n_lo, 2 * KT)
        pool.memset(xqb[:, :, :, :], 0.0).then_inc(qbd_z, 1)
        for j in range(SLOT_CO, SLOTS):
            kind, g, q = ffn_slot(j - SLOT_F) if j >= SLOT_F else ("co", 0, 0)
            if j == SLOT_F:
                pool.wait_ge(n_lo, 3 * KT)
                for e in ue:
                    ins = pool.memset(e[:, 0:2], 0.0)
                ins.then_inc(f_c, 6)
            split(j)
            if (kind, q) == ("up", 0) and g >= 1 or (kind, g, q) == ("down", NG - 1, 0):
                g = g - 1 if kind == "up" else g
                for i in range(2):
                    pool.wait_ge(ghi, 2 * g + i + 1)
                    if g >= 2:
                        pool.wait_ge(g_done, DOWN_END[g - 2])
                    pool.tensor_tensor(gl[g % 2][:, i, :], uy[2 * i + 1][:, :], gh[g % 2][:, i, :].bitcast(F32),
                                       ALU.subtract).then_inc(glo, 1)

    @block.scalar
    def _(act):
        self_ = Chain(act, act_self)
        act.wait_ge(par_t, 1)
        act.activation(vec[:, :], ps[:, 7, 0:52], ACT.Copy)
        act.activation(cw[:, :], ps[:, 7, 64:64 + CW * CT], ACT.Copy).then_inc(par_c, 1)
        act.wait_ge(par_t, 2)
        act.activation(fw[:, :, :], ps[:, 6, 0:4 * 2 * FT].rearrange("p (j c) -> p j c", j=4), ACT.Copy).then_inc(par_c, 1)
        act.wait_ge(par_t, 3)
        act.activation(cf[:, 0:5, :, :], ps[:, 5, 0:5 * 88].rearrange("p (b j c) -> p b j c", b=5, j=2), ACT.Copy)
        act.activation(cf[:, 5:8, :, :], ps[:, 4, 0:3 * 88].rearrange("p (b j c) -> p b j c", b=3, j=2), ACT.Copy).then_inc(par_c, 1)
        for h in range(NH):
            act.wait_ge(tp_t, h + 1)
            act.activation(tst[:, h, :], ps[:, 5 + h % 2, 0:384], ACT.Copy).then_inc(tp_c, 1)
        act.wait_ge(tp_c, NH)
        act.dma_start(toep_d, tst[:, :, :].rearrange("p h i -> p (h i)")).then_inc(toep_out, 16)
        for n in range(2 * NB):
            t, g = divmod(n, 2)
            act.wait_ge(xt_t, n + 1)
            act.activation(xT[:, 4 * g:4 * g + 4, t * P:(t + 1) * P],
                           ps[:, n % 3, :].rearrange("p (k n) -> p k n", k=4), ACT.Copy).then_inc(xt_c, 1)
        act.wait_ge(xt_t, 2 * NB + 1)
        act.activation(xT[:, :, S:T], ps[:, 2 * NB % 3, 0:64].rearrange("p (k n) -> p k n", k=8), ACT.Copy).then_inc(xt_c, 1)

        def squares(i):
            for k in range(KT):
                n = KT * i + k
                if n == 0:
                    act.wait_ge(xt_c, 2 * NB + 1)
                    act.wait_ge(toep_out, 16)
                if n >= 2:
                    act.wait_ge(n_acc, n - 1)
                if i:
                    act.wait_ge(res_c, RES_AT[i] + 3 * (k + 1))
                act.activation(nsq[n % 2][:, :], xT[:, k, :], ACT.Square).then_inc(n_sq, 1)

        def norm(i):
            if i < 3:
                squares(i)
            act.wait_ge(n_var, i + 1)
            act.activation(nr[:, :], nr[:, :], ACT.Sqrt).then_inc(n_rstd, 1)

        def norm_hi(i):
            for k in range(KT):
                act.wait_ge(n_h, KT * i + k + 1)
                act.activation(hh[:, k, :], nh_[k % 2][:, :], ACT.Copy).then_inc(n_hi, 1)

        for n in range(4):
            act.wait_ge(mt_t, n + 1)
            t, g = divmod(n, 2)
            act.activation(memT[:, 4 * g:4 * g + 4, t * P:(t + 1) * P],
                           ps[:, 3 + n % 2, :].rearrange("p (k n) -> p k n", k=4), ACT.Copy).then_inc(mt_c, 1)
        act.wait_ge(mt_c, 4)
        act.activation(msq[:, :, :], memT[:, :, :], ACT.Square).then_inc(m_sq, 1)
        act.wait_ge(m_var, 1)
        act.activation(mr[:, :], mr[:, :], ACT.Sqrt).then_inc(m_rstd, 1)
        act.wait_ge(m_h, 1)
        act.activation(mhh[:, :, :], memT[:, :, :], ACT.Copy).then_inc(m_hi, 1)
        for j in range(4):
            act.wait_ge(g_done, j + 1)
            dst = kmT[:, j, :] if j < 2 else mvT[:, j - 2, :]
            act.activation(dst, ps[:, 5 + j % 2, 0:NM], ACT.Copy).then_inc(ckv_c, 1)
        for t in range(2):
            act.wait_ge(mkv_t, t + 1)
            act.activation(mtk[:, t, :], ps[:, 3 + t, :], ACT.Copy).then_inc(mkv_c, 1)
            act.activation(vm[:, t, :], ps[:, 3 + t, NM:2 * NM], ACT.Copy).then_inc(mkv_c, 1)
        act.wait_ge(mkv_c, 4)
        act.dma_start(o["mem_k_prompt"][0, 0].rearrange("(t p) h d -> p t (h d)", p=P), mtk[:, :, 0:NM]).then_inc(mem_out, 16)
        act.dma_start(o["mem_v_prompt"][0, 0].rearrange("(t p) h d -> p t (h d)", p=P), mtk[:, :, NM:2 * NM]).then_inc(mem_out, 16)
        norm(0)
        norm_hi(0)
        act.wait_ge(mem_out, 32)
        act.wait_ge(spilled, 16)
        n_aux, n_ktok = 0, 0

        def unit_from(js, c):
            kind, m, _, _ = IN_SLOTS[js]
            cols = slice(c * CH, (c + 1) * CH)
            act.wait_ge(g_done, UNITS_TO[SLOT_IN + js] + c + 1)
            src = ps[:, 3 * (js % 2) + c, 0:CH]
            if kind == "qi" or kind == "q":
                act.activation(qx[:, m, cols], src, ACT.Copy).then_inc(in_c, 1)
            elif kind == "kw":
                act.activation(kw[:, cols], ps[0:72, 3 * (js % 2) + c, 0:CH], ACT.Copy).then_inc(in_c, 1)
            elif kind == "k":
                act.activation(kT_[:, m, cols], src, ACT.Copy).then_inc(in_c, 1)
            elif kind == "v":
                if m == 0 and c == 0:
                    act.wait_ge(ki_out, 32)
                act.activation(vT1[:, cols], src, ACT.Copy).then_inc(in_c, 1)
            elif kind == "ga":
                if m:
                    act.wait_ge(u_ok, 3 * (m - 1) + c + 1)
                act.activation(ga[:, cols], src, ACT.Copy).then_inc(in_c, 1)
            else:
                if 3 * m + c >= 2:
                    act.wait_ge(u_ok, 3 * m + c - 1)
                act.wait_ge(in_c, 3 * js)
                act.activation(gb[(3 * m + c) % 2][:, :], src, ACT.Sigmoid).then_inc(gb_ok, 1)
                act.wait_ge(gb_ok, 3 * m + c + 1)
                act.sem_inc(in_c, 1)

        def aux(n):
            act.wait_ge(aux_t, n + 1)
            return ps[:, 6 + n % 2, :]

        def tokens_out(kv, m):
            nonlocal n_aux, n_ktok
            r, buf = n_ktok % 2, ks[n_ktok % 2]
            if n_ktok >= 2:
                act.wait_ge(kv_out[r], 16 * (n_ktok // 2))
            for g in range(2):
                act.activation(buf[:, 4 * g:4 * g + 4, :], aux(n_aux).rearrange("p (t n) -> p t n", t=4),
                               ACT.Copy).then_inc(aux_c, 1)
                n_aux += 1
            act.activation(ksm[:, kv, m * P:(m + 1) * P], aux(n_aux)[0:DB, 0:P], ACT.Copy).then_inc(aux_c, 1)
            n_aux += 1
            act.wait_ge(aux_c, n_aux)
            dst = o["v_prompt" if kv else "k_prompt"][0, 0].rearrange("(t p) h d -> p t (h d)", p=P)
            act.dma_start(dst[:, :, m * P:(m + 1) * P], buf[:, :, :]).then_inc(kv_out[r], 16)
            n_ktok += 1

        for kind, i in order_of_w_in():
            if kind == "slot":
                for c in range(3):
                    unit_from(i, c)
                if i == 4:
                    act.wait_ge(in_c, 15)
                    act.dma_start(ki2[64:128, :], kw[0:64, :]).then_inc(ki_dup, 16)
                    act.wait_ge(wsel_ok, 1)
                    for h in range(NH):
                        lo = 64 * (h % 2)
                        act.activation(qis[:, :, h], qx[lo:lo + DH, h // 2, S:T], ACT.Copy)
                    flat = wsel[:, :, :].rearrange("h b c -> h (b c)")
                    act.activation(flat[:, 0:64:9], kw[64:72, S:T], ACT.Copy, scale=R8).then_inc(wsel_ok, 1)
            elif kind == "ki":
                for g in range(3):
                    src = aux(n_aux)
                    if g < 2:
                        v4 = src.rearrange("p (t n) -> p t n", t=4)
                        act.activation(kit[:, 4 * g:4 * g + 4, :], v4[:, :, 0:DH], ACT.Copy)
                        act.activation(wj[:, 4 * g:4 * g + 4, :], v4[:, :, DH:72], ACT.Copy, scale=R8).then_inc(aux_c, 1)
                    else:
                        act.activation(kism[:, :], src[0:DB, 0:DH], ACT.Copy).then_inc(aux_c, 1)
                    n_aux += 1
                act.wait_ge(aux_c, n_aux)
                act.dma_start(o["idx_k_prompt"][0, 0].rearrange("(t p) d -> p t d", p=P), kit[:, :, :]).then_inc(ki_out, 16)
                act.dma_start(o["idx_k_sample"][0, :, 0, :], kism[:, :]).then_inc(ki_out, 16)
            elif kind == "idx":
                for n, (b, h, f, w) in enumerate(IDX_UNITS):
                    if b == i:
                        if n >= 2:
                            act.wait_ge(idx_c, n - 1)
                        act.activation(rr[n % 2][:, 0:w], aux(n_aux)[:, 0:w], ACT.Relu, scale=DH ** -0.5).then_inc(aux_c, 1)
                        n_aux += 1
            elif kind == "ktok":
                tokens_out(0, i)
            elif kind == "vtok":
                tokens_out(1, i)
            else:
                act.dma_start(o["k_sample"][0, :, 0].rearrange("b h d -> b (h d)"), ksm[:, 0, :]).then_inc(ksm_out, 16)
                act.dma_start(o["v_sample"][0, :, 0].rearrange("b h d -> b (h d)"), ksm[:, 1, :]).then_inc(ksm_out, 16)
                act.activation(cpt[:, :], aux(n_aux)[0:HALO, :], ACT.Copy).then_inc(aux_c, 1)
                act.activation(cst[:, :], aux(n_aux + 1)[0:DB, :], ACT.Copy).then_inc(aux_c, 1)
                n_aux += 2
                act.wait_ge(aux_c, n_aux)
                act.dma_start(o["conv_prompt"][0, 0], cpt[:, :]).then_inc(conv_out, 16)
                act.dma_start(o["conv_sample"][0, :, HALO - 1, :], cst[:, :]).then_inc(conv_out, 16)
                for g in range(2):
                    src = aux(n_aux)
                    for m in range(CT):
                        mm = act.activation(us[:, m, 4 * g:4 * g + 4, 0:HALO],
                                            src[:, m * 120:(m + 1) * 120].rearrange("p (b j) -> p b j", b=4), ACT.Copy)
                    mm.then_inc(aux_c, 1)
                    n_aux += 1
        act.activation(kws[:, :], kw[:, S:T], ACT.Copy)
        act.wait_ge(ksm_out, 32)
        act.wait_ge(conv_out, 48)
        for r in range(2):
            act.wait_ge(kv_out[r], 64)
        for m in range(CT):
            act.wait_ge(ln_c, m + 1)
            if m >= 2:
                act.wait_ge(ln_ss, m - 1)
            act.activation(lq[m % 2][:, :], y[:, m, :], ACT.Square).then_inc(ln_sq, 1)
        act.wait_ge(ln_var, 1)
        act.activation(lr[:, :], lr[:, :], ACT.Sqrt).then_inc(ln_rstd, 1)
        for m in range(CT):
            act.wait_ge(ln_h, m + 1)
            act.activation(lh[m % 2][:, :], lh[m % 2][:, :], ACT.Silu, scale=vec[:, 44 + m:45 + m],
                           bias=vec[:, 48 + m:49 + m]).then_inc(ln_act, 1)
            act.wait_ge(ln_act, m + 1)
            act.activation(hh[:, CT + m, :], lh[m % 2][:, :], ACT.Copy).then_inc(ln_hi, 1)
        for i in range(len(ITEMS) + 8):
            if i < len(ITEMS):
                b, h = ITEMS[i]
                row = lg[i % 2][:, 0:P * (b + 1)]
                act.wait_ge(mx_ok, i + 1)
                if h == 0 and b >= 2:
                    act.wait_ge(att_ok, b - 1)
                act.activation(row, row, ACT.Exp, bias=mx[:, i % 4, 2:3], scale=DH ** -0.5,
                               accum_out=rs[:, b % 2, h:h + 1]).then_inc(exp_ok, 1)
            if 2 <= i < len(ITEMS) + 2:
                n = i - 2
                k = min(ITEMS[n][0] + 1, 4)
                act.wait_ge(t0_t, n + 1)
                if n >= 2:
                    act.wait_ge(pv, n - 1)
                act.activation(pt[n % 2][:, 0:k, :], ps[:, 4, 0:k * P].rearrange("p (k n) -> p k n", k=k),
                               ACT.Copy).then_inc(t0_c, 1)
            if i >= 14 and (i - 14) % 8 == 0:
                b = (i - 14) // 8
                act.wait_ge(aT_t, b + 1)
                act.activation(hh[:, 0:CT, b * P:(b + 1) * P], ps[:, 7, :].rearrange("p (m n) -> p m n", m=CT),
                               ACT.Copy).then_inc(aT_hi, 1)
        act.wait_ge(aT_lo, NB)
        for b in range(DB + 1):
            if b < DB:
                act.wait_ge(si_t, b + 1)
                if b >= 2:
                    act.wait_ge(si_s, b - 1)
                act.activation(kis[b % 2][:, :], ps[0:DH, b % 2, :], ACT.Copy).then_inc(si_c, 1)
            if b >= 1:
                n = b - 1
                act.wait_ge(si_s, n + 1)
                if n >= 2:
                    act.wait_ge(si_w, n - 1)
                act.activation(rsm[n % 2][:, 0:PAST], ps[0:NH, 2 + n % 2, :], ACT.Relu, scale=DH ** -0.5)
                act.activation(rsm[n % 2][:, PAST:KEYS], ps[0:NH, 4 + 3 * (n % 2), 0:1], ACT.Relu, scale=DH ** -0.5).then_inc(si_r, 1)
        for n in range(DB * NPG):
            act.wait_ge(sk_t, n + 1)
            if n >= 2:
                act.wait_ge(sk_s, n - 1)
            act.activation(kpt[n % 2][:, :, :], ps[:, n % 2, :].rearrange("p (m n) -> p m n", m=CT), ACT.Copy).then_inc(sk_c, 1)
        act.wait_ge(sk_s, DB * NPG)
        act.activation(sl[:, :, :], ps[:, 7, 0:256].rearrange("p (j n) -> p j n", j=NPG), ACT.Copy).then_inc(sl_c, 1)
        act.wait_ge(sb_t, 1)
        act.activation(adds[:, 0:PAST], ps[0:64, 5, :], ACT.Copy)
        act.activation(adds[:, PAST:KEYS], ps[0:64, 6, 0:1], ACT.Copy).then_inc(sb_c, 1)
        act.wait_ge(s_nm, 1)
        act.activation(ls[:, :], ls[:, :], ACT.Exp, bias=ssm[:, 3:4], scale=DH ** -0.5, accum_out=ssm[:, 4:5]).then_inc(s_exp, 1)
        act.wait_ge(sp_t, 1)
        act.activation(spT[:, :, :], ps[:, 0, 0:256].rearrange("p (j n) -> p j n", j=NPG), ACT.Copy)
        act.activation(pdT[:, :], ps[0:8, 1, 0:64], ACT.Copy).then_inc(sp_c, 1)
        act.wait_ge(s_att, 1)
        act.activation(hh[:, 0:CT, S:T], aself[:, :, :], ACT.Copy).then_inc(s_hi, 1)
        norm(1)
        norm_hi(1)
        for n in range(6):
            act.wait_ge(g_done, UNITS_TO[SLOT_CQ] + n + 1)
            m, c = divmod(n, 3)
            act.activation(qc[:, m, c * CH:(c + 1) * CH], ps[:, n % 6, 0:CH], ACT.Copy).then_inc(qc_c, 1)
        for i in range(NB + 2):
            if i < NB:
                act.wait_ge(mx_ok, N_ITEMS + i + 1)
                if i >= 2:
                    act.wait_ge(t1_t, N_LATE + i - 1)
                    act.wait_ge(att_ok, NB + i - 1)
                for h in range(MH):
                    ins = act.activation(xp[i % 2][:, h, :], ps[:, 2 * (i % 2) + h % 2, h // 2 * NM:(h // 2 + 1) * NM], ACT.Exp,
                                         bias=xm[:, i % 2, 0, h:h + 1], scale=DH ** -0.5, accum_out=xm[:, i % 2, 1, h:h + 1])
                ins.then_inc(exp_ok, 1)
            if 1 <= i < NB + 1:
                n = i - 1
                act.wait_ge(t0_t, N_ITEMS + n + 1)
                if n >= 2:
                    act.wait_ge(pv, N_ITEMS + n - 1)
                act.activation(xpt[n % 2][:, 0:4, :], ps[:, 4, :].rearrange("p (k n) -> p k n", k=4), ACT.Copy).then_inc(t0_c, 1)
            if i >= 2:
                n = i - 2
                act.wait_ge(aT_t, NB + n + 1)
                act.activation(xh[:, :, n * P:(n + 1) * P], ps[:, 7, 0:2 * P].rearrange("p (m n) -> p m n", m=2), ACT.Copy).then_inc(aT_hi, 1)
        act.wait_ge(aT_lo, NB + NB)
        for b in range(DB):
            act.wait_ge(sk_t, N_PAGES + b + 1)
            if b >= 2:
                act.wait_ge(sk_s, N_PAGES + b - 1)
            act.activation(xkt[b % 2][:, :, :, :].rearrange("p t m n -> p (t m n)"), ps[:, b % 2, :], ACT.Copy).then_inc(sk_c, 1)
        act.wait_ge(sk_s, N_PAGES + DB)
        act.activation(xsl[:, :, :], ps[:, 2, 0:64].rearrange("p (t n) -> p t n", t=2), ACT.Copy).then_inc(sl_c, 1)
        act.wait_ge(s_nm, 2)
        act.activation(xls[:, :], ps[0:32, 3, 0:NM], ACT.Exp, bias=xss[:, 1:2], scale=DH ** -0.5, accum_out=xss[:, 2:3]).then_inc(s_exp, 1)
        act.wait_ge(sp_t, 2)
        act.activation(xsp[:, :, :], ps[:, 4, 0:64].rearrange("p (t n) -> p t n", t=2), ACT.Copy).then_inc(sp_c, 1)
        act.wait_ge(s_att, 2)
        act.activation(xh[:, :, S:T], xas[:, :, :], ACT.Copy).then_inc(s_hi, 1)
        norm(2)
        norm_hi(2)

        def up(g, i=None):
            first = i is None
            for q in range(4):
                tile = up_tile(g, q)
                e, y_ = ue[q % 2], uy[q]
                for c in range(3):
                    cols = slice(c * CH, (c + 1) * CH)
                    src = ps[:, 3 * (q % 2) + c, 0:CH]
                    act.wait_ge(g_done, (FFN0 if first else FFN0 + 36 * g - 24) + 3 * q + c + 1)
                    if not first or q >= 2:
                        act.wait_ge(cv, 4 * g + q - 1)
                    if not first:
                        act.wait_ge(glo, 2 * g - 1 + q // 2)
                    act.activation(e[:, 2 + c * CH:2 + (c + 1) * CH], src, ACT.Copy)
                    ins = act.activation(y_[:, cols], src, ACT.Identity, scale=fw[:, 2, bass.ds(tile, 1)], bias=fw[:, 3, bass.ds(tile, 1)])
                    if c == 2:
                        ins = act.activation(upl[:, :, bass.ds(tile, 1)], ps[:, 3 * (q % 2) + 2, CH - 10:CH].unsqueeze(2), ACT.Copy)
                    ins.then_inc(f_c, 1)
                if q % 2:
                    t = q // 2
                    act.wait_ge(cv, 4 * g + q)
                    act.activation(uy[q - 1][:, :], uy[q - 1][:, :], ACT.Silu).then_inc(slu, 1)
                    act.wait_ge(prd, 2 * g + t + 1)
                    if not first:
                        act.wait_ge(g_done, FFN0 + 36 * g - 24)
                    act.activation(gh[i or 0][:, t, :], uy[q][:, :], ACT.Copy).then_inc(ghi, 1)

        up(0)
        with act.Fori(0, (NG - 1) // 2) as i:
            up(2 * i + 1, 1)
            up(2 * i + 2, 0)
        squares(3)
        for q in range(2):
            act.wait_ge(fo_t, q + 1)
            n = 4 if q == 0 else 1
            act.activation(fst[:, 4 * q:4 * q + n, :], ps[0:88, 3 + q, 0:n * P].rearrange("p (k n) -> p k n", k=n), ACT.Copy).then_inc(fo_c, 1)
        norm(3)
        for t in range(NB + 1):
            act.wait_ge(yo_t, 2 * t + 1)
            if t >= 2:
                act.wait_ge(y_out[t % 2], 16 * (t // 2))
            rows = P if t < NB else DB
            act.activation(ytk[t % 2][0:rows, 0:512], ps[0:rows, 3 + 2 * (t % 2), :], ACT.Copy).then_inc(yo_a, 1)

    @block.vector
    def _(dve):
        self_ = Chain(dve, dve_self)

        def norm(i, gain, residual=None):
            for k in range(KT):
                n = KT * i + k
                if residual:
                    residual(k)
                dve.wait_ge(n_sq, n + 1)
                if k == 0:
                    dve.tensor_copy(nr[:, :], nsq[n % 2][:, :]).then_inc(n_acc, 1)
                else:
                    dve.wait_ge(n_acc, n)
                    dve.tensor_tensor(nr[:, :], nr[:, :], nsq[n % 2][:, :], ALU.add).then_inc(n_acc, 1)
            dve.wait_ge(n_ss, i + 1)
            self_.link(dve.tensor_scalar(nr[:, :].rearrange("p (c n) -> p c n", c=3), ps[:, 0:3, 0:CH],
                                         1.0 / D, RMS_EPS, ALU.mult, ALU.add))
            dve.reciprocal(nr[:, :], nr[:, :]).then_inc(n_var, 1)
            dve.wait_ge(n_rstd, i + 1)
            if i == 3:
                for k in range(KT):
                    dve.scalar_tensor_tensor(out=yT[:, k, :], in0=xT[:, k, :], scalar=vec[:, gain + k:gain + k + 1],
                                             in1=nr[:, :], op0=ALU.mult, op1=ALU.mult).then_inc(n_h, 1)
                return
            for k in range(KT):
                n = KT * i + k
                if k >= 2:
                    dve.wait_ge(n_hi, n - 1)
                    dve.wait_ge(n_lo, n - 1)
                dve.scalar_tensor_tensor(out=nh_[k % 2][:, :], in0=xT[:, k, :], scalar=vec[:, gain + k:gain + k + 1],
                                         in1=nr[:, :], op0=ALU.mult, op1=ALU.mult).then_inc(n_h, 1)
                if k >= 1:
                    norm_lo(n - 1)
            norm_lo(KT * i + KT - 1)

        def norm_lo(n):
            k = n % KT
            dve.wait_ge(n_hi, n + 1)
            dve.tensor_tensor(hl[:, k, :], nh_[k % 2][:, :], hh[:, k, :].bitcast(F32), ALU.subtract).then_inc(n_lo, 1)

        dve.wait_ge(par_in, 16 * NPAR)
        dve.tensor_copy(rbx[:, :, :], rbt[:, :].unsqueeze(2).to_broadcast([32, NH, P])).then_inc(rbx_ok, 1)
        dve.wait_ge(m_sq, 1)
        dve.tensor_reduce(mr[:, :], msq[:, :, :].rearrange("p k t -> p t k"), AX.X, ALU.add).then_inc(m_ss, 1)
        dve.wait_ge(m_ss, 2)
        self_.link(dve.tensor_scalar(mr[:, :], ps[:, 7, 0:NM], 1.0 / D, RMS_EPS, ALU.mult, ALU.add))
        dve.reciprocal(mr[:, :], mr[:, :]).then_inc(m_var, 1)
        dve.wait_ge(m_rstd, 1)
        for k in range(KT):
            last = dve.scalar_tensor_tensor(out=memT[:, k, :], in0=memT[:, k, :], scalar=vec[:, 16 + k:17 + k],
                                            in1=mr[:, :], op0=ALU.mult, op1=ALU.mult)
        last.then_inc(m_h, 1)
        dve.wait_ge(m_hi, 1)
        dve.tensor_tensor(mhl[:, :, :], memT[:, :, :], mhh[:, :, :].bitcast(F32), ALU.subtract).then_inc(m_lo, 1)
        dve.wait_ge(toep_out, 16)
        norm(0, 0)
        for n, (b, h, f, w) in enumerate(IDX_UNITS):
            dst = sc[:, IDX_AT[b] + 512 * f:IDX_AT[b] + 512 * f + w]
            dve.wait_ge(aux_c, IDX_AUX[n])
            if h == 0:
                dve.tensor_scalar(dst, rr[n % 2][:, 0:w], wj[:, b, 0:1], None, ALU.mult).then_inc(idx_c, 1)
            else:
                dve.wait_ge(idx_c, n + 1 - (-(-IDX_EXT[b] // 512)))
                dve.scalar_tensor_tensor(out=dst, in0=rr[n % 2][:, 0:w], scalar=wj[:, b, h:h + 1], in1=dst,
                                         op0=ALU.mult, op1=ALU.add).then_inc(idx_c, 1)
        dve.wait_ge(idx_c, len(IDX_UNITS))
        for b in range(2, NB):
            diag = sc[:, IDX_AT[b] + P * b:IDX_AT[b] + P * (b + 1)]
            mm = dve.scalar_tensor_tensor(out=diag, in0=causal[:, :], scalar=CAUSAL / NEG, in1=diag, op0=ALU.mult, op1=ALU.add)
        self_.link(mm)
        for b in range(2, NB):
            row = sc[:, IDX_AT[b]:IDX_AT[b] + IDX_EXT[b]]
            for _ in range(TOPK // 8):
                self_.link(dve.max(s8[:, :], row))
                self_.link(dve.match_replace(row, s8[:, :], row, REPLACED))
            self_.link(dve.tensor_scalar(row, row, TAKEN, NEG, ALU.is_gt, ALU.mult))
        dve.wait_ge(u_ok, 3 * CT)
        dve.wait_ge(g_done, UNITS_TO[SLOT_O])
        for m in range(CT):
            dve.tensor_scalar(y[:, m, 0:S], u[:, m, 0:S], cw[:, m:m + 1], vec[:, 40 + m:41 + m], ALU.mult, ALU.add).then_inc(tap, 1)
        with dve.Fori(1, CW) as j:
            for m in range(CT):
                dve.wait_ge(tap, CT * j + (m + 1 - CT))
                dve.scalar_tensor_tensor(out=y[:, m, 0:S], in0=u[:, m, bass.ds(j, S)],
                                         scalar=cw[:, bass.ds(CT * j + m, 1)], in1=y[:, m, 0:S],
                                         op0=ALU.mult, op1=ALU.add).then_inc(tap, 1)
        dve.wait_ge(aux_c, AUX_IN)
        taps = cw[:, :].rearrange("p (j m) -> p m j", m=CT)
        for m in range(CT):
            mm = dve.tensor_tensor(us[:, m, :, :], us[:, m, :, :], taps[:, m, :].unsqueeze(1).to_broadcast([P, DB, CW]), ALU.mult)
        self_.link(mm)
        for m in range(CT):
            mm = dve.tensor_reduce(usr[:, m, :], us[:, m, :, :], AX.X, ALU.add)
        self_.link(mm)
        for m in range(CT):
            mm = dve.tensor_scalar(y[:, m, S:T], usr[:, m, :], vec[:, 40 + m:41 + m], None, ALU.add)
        mm.then_inc(y_ok, 1)
        c3 = lambda x: x.rearrange("p (c n) -> p c n", c=3)
        dve.wait_ge(ln_s, 1)
        dve.wait_ge(y_ok, 1)
        dve.wait_ge(tap, CT * CW)
        for m in range(CT):
            dve.scalar_tensor_tensor(out=c3(y[:, m, :]), in0=ps[:, 0:3, 0:CH], scalar=-1.0 / DA, in1=c3(y[:, m, :]),
                                     op0=ALU.mult, op1=ALU.add).then_inc(ln_c, 1)
        dve.wait_ge(ln_ss, CT)
        self_.link(dve.tensor_scalar(c3(lr[:, :]), ps[:, 3:6, 0:CH], 1.0 / DA, LN_EPS, ALU.mult, ALU.add))
        dve.reciprocal(lr[:, :], lr[:, :]).then_inc(ln_var, 1)
        dve.wait_ge(ln_rstd, 1)

        def ln_low(m):
            dve.wait_ge(ln_hi, m + 1)
            dve.tensor_tensor(hl[:, CT + m, :], lh[m % 2][:, :], hh[:, CT + m, :].bitcast(F32), ALU.subtract).then_inc(ln_lo, 1)

        for m in range(CT):
            if m >= 2:
                dve.wait_ge(ln_lo, m - 1)
            dve.tensor_tensor(lh[m % 2][:, :], y[:, m, :], lr[:, :], ALU.mult).then_inc(ln_h, 1)
            if m >= 1:
                ln_low(m - 1)
        dve.wait_ge(ln_h, CT)
        ln_low(CT - 1)
        for i in range(len(ITEMS) + 9):
            if i < len(ITEMS):
                b, h = ITEMS[i]
                k0, ext = max(0, P * (b - 1)), P * (b + 1)
                dve.wait_ge(qk, i + 1)
                if i >= 2:
                    dve.wait_ge(t0_t, i - 1)
                    if late(i - 1):
                        dve.wait_ge(t1_t, late(i - 1))
                if i >= 4:
                    dve.wait_ge(exp_ok, i - 3)
                if h == 0:
                    dve.wait_ge(nb_ok, b - 1) if b >= 2 else dve.wait_ge(bt_ok, 1)
                add = nb[:, h, :] if b >= 2 else bt[:, h, P * (1 - b):2 * P]
                ins = dve.tensor_tensor_reduce(out=lg[i % 2][:, k0:ext], in0=pair(i)[:, k0:ext], in1=add, scale=1.0, scalar=CAUSAL,
                                               op0=ALU.add, op1=ALU.max, accum_out=mx[:, i % 4, 0:1])
                if b >= 2:
                    ins = dve.tensor_tensor_reduce(out=lg[i % 2][:, 0:k0], in0=pair(i)[:, 0:k0],
                                                   in1=sc[:, IDX_AT[b]:IDX_AT[b] + k0], scale=1.0, scalar=CAUSAL,
                                                   op0=ALU.add, op1=ALU.max, accum_out=mx[:, i % 4, 1:2])
                ins.then_inc(added, 1)
                dve.wait_ge(added, i + 1)
                far = mx[:, i % 4, 1:2] if b >= 2 else mx[:, i % 4, 0:1]
                dve.tensor_scalar(mx[:, i % 4, 2:3], mx[:, i % 4, 0:1], far, -DH ** -0.5, ALU.max, ALU.mult).then_inc(mx_ok, 1)
            if 2 <= i < len(ITEMS) + 2 and ITEMS[i - 2][0] >= 4:
                n = i - 2
                k = ITEMS[n][0] + 1 - 4
                dve.wait_ge(t1_t, late(n + 1))
                dve.wait_ge(pv, n - 1)
                dve.tensor_copy(pt[n % 2][:, 4:4 + k, :], ps[:, 5, 0:k * P].rearrange("p (k n) -> p k n", k=k)).then_inc(t1_c, 1)
            if i >= 11 and (i - 11) % 8 == 0:
                b = (i - 11) // 8
                dve.wait_ge(exp_ok, NH * (b + 1))
                self_.link(dve.reciprocal(ri[:, b % 2, :], rs[:, b % 2, :]))
                dve.wait_ge(pv, NH * (b + 1))
                if b >= 1:
                    dve.wait_ge(aT_t, b)
                dve.tensor_tensor(att[:, :].rearrange("p (h d) -> p h d", h=NH), ps[:, 6, :].rearrange("p (h d) -> p h d", h=NH),
                                  ri[:, b % 2, :].unsqueeze(2).to_broadcast([P, NH, DH]), ALU.mult).then_inc(att_ok, 1)
            if i >= 16 and (i - 16) % 8 == 0:
                b = (i - 16) // 8
                dve.wait_ge(aT_hi, b + 1)
                dve.tensor_tensor(hl[:, 0:CT, b * P:(b + 1) * P], ps[:, 7, :].rearrange("p (m n) -> p m n", m=CT),
                                  hh[:, 0:CT, b * P:(b + 1) * P].bitcast(F32), ALU.subtract).then_inc(aT_lo, 1)
        dve.wait_ge(aT_lo, NB)
        dve.wait_ge(qbd_z, 1)
        for m in range(CT):
            for e in range(2):
                ins = dve.tensor_copy(qbd[64 * e:64 * e + 64, m, :, 2 * m + e], qx[64 * e:64 * e + 64, m, S:T])
        ins.then_inc(qbd_ok, 1)
        dve.wait_ge(srb_in, 32)
        dve.tensor_copy(srb[:, :, :], srb1[:, :].unsqueeze(1).to_broadcast([32, DB, NH])).then_inc(srb_ok, 1)
        dve.wait_ge(si_w, DB)
        dve.tensor_copy(ssc[:, 0:PAST], ps[0:DB, 5, :])
        self_.link(dve.tensor_copy(ssc[:, PAST:KEYS], ps[0:DB, 6, 0:1]))
        for _ in range(TOPK_S // 8):
            self_.link(dve.max(s8[0:DB, :], ssc[:, :]))
            self_.link(dve.match_replace(ssc[:, :], s8[0:DB, :], ssc[:, :], REPLACED))
        dve.tensor_scalar(ssc[:, :], ssc[:, :], TAKEN, NEG, ALU.is_gt, ALU.mult).then_inc(smask, 1)
        dve.wait_ge(sb_c, 1)
        dve.wait_ge(sl_t, 1)
        dve.tensor_tensor_reduce(out=ls[:, 0:PAST], in0=ps[0:64, 4, :], in1=adds[:, 0:PAST], scale=1.0, scalar=CAUSAL,
                                 op0=ALU.add, op1=ALU.max, accum_out=ssm[:, 0:1])
        self_.link(dve.tensor_tensor_reduce(out=sself[:, :], in0=ps[0:64, 3, 0:8], in1=same[:, :], scale=1.0, scalar=0.0,
                                            op0=ALU.mult, op1=ALU.add, accum_out=ssm[:, 1:2]))
        self_.link(dve.tensor_tensor(ls[:, PAST:KEYS], adds[:, PAST:KEYS], ssm[:, 1:2], ALU.add))
        dve.tensor_scalar(ssm[:, 3:4], ls[:, PAST:KEYS], ssm[:, 0:1], -DH ** -0.5, ALU.max, ALU.mult).then_inc(s_nm, 1)
        dve.wait_ge(s_exp, 1)
        self_.link(dve.reciprocal(ssm[:, 5:6], ssm[:, 4:5]))
        self_.link(dve.tensor_scalar(ls[:, :], ls[:, :], ssm[:, 5:6], None, ALU.mult))
        dve.tensor_scalar(pd[:, :], same[:, :], ls[:, PAST:KEYS], None, ALU.mult).then_inc(s_p, 1)
        dve.wait_ge(sv_t, DB)
        heads = ps[:, 7, 256:512].rearrange("p (m b h) -> p m b h", m=CT, b=DB)
        for m in range(CT):
            for e in range(2):
                ins = dve.tensor_copy(aself[64 * e:64 * e + 64, m, :], heads[64 * e:64 * e + 64, m, :, 2 * m + e])
        ins.then_inc(s_att, 1)
        dve.wait_ge(s_hi, 1)
        dve.tensor_tensor(hl[:, 0:CT, S:T], aself[:, :, :], hh[:, 0:CT, S:T].bitcast(F32), ALU.subtract).then_inc(s_lo, 1)
        dve.sem_inc(res_c, 6)
        dve.wait_ge(x_back, 16)

        def add_to_x(m, unit, bank, count):
            for c in range(3):
                cols = slice(c * CH, (c + 1) * CH)
                dve.wait_ge(g_done, unit + c + 1)
                dve.tensor_tensor(xT[:, m, cols], xT[:, m, cols], ps[:, bank + c, 0:CH], ALU.add).then_inc(res_c, 1)

        norm(1, 8, lambda k: add_to_x(k, UNITS_TO[SLOT_O + k], 3 * (k % 2), 0))
        for i in range(NB + 3):
            if i < NB:
                dve.wait_ge(qk, N_ITEMS + i + 1)
                if i >= 2:
                    dve.wait_ge(exp_ok, N_ITEMS + i - 1)
                rows = ps[:, 2 * (i % 2):2 * (i % 2) + 2, :].rearrange("p a (h n) -> p a h n", h=2)
                self_.link(dve.tensor_reduce(xm[:, i % 2, 0, :].rearrange("p (h a) -> p a h", a=2), rows, AX.X, ALU.max))
                dve.tensor_scalar(xm[:, i % 2, 0, :], xm[:, i % 2, 0, :], -DH ** -0.5, None, ALU.mult).then_inc(mx_ok, 1)
            if 1 <= i < NB + 1:
                n = i - 1
                dve.wait_ge(t1_t, N_LATE + n + 1)
                if n >= 2:
                    dve.wait_ge(pv, N_ITEMS + n - 1)
                dve.tensor_copy(xpt[n % 2][:, 4:8, :], ps[:, 5, :].rearrange("p (k n) -> p k n", k=4)).then_inc(t1_c, 1)
                self_.link(dve.reciprocal(xm[:, n % 2, 2, :], xm[:, n % 2, 1, :]))
                dve.wait_ge(pv, N_ITEMS + n + 1)
                if n >= 1:
                    dve.wait_ge(aT_t, NB + n)
                dve.tensor_tensor(xa[:, :].rearrange("p (h d) -> p h d", h=MH), ps[:, 6, 0:256].rearrange("p (h d) -> p h d", h=MH),
                                  xm[:, n % 2, 2, :].unsqueeze(2).to_broadcast([P, MH, DH]), ALU.mult).then_inc(att_ok, 1)
            if 2 <= i < NB + 2:
                n = i - 2
                dve.wait_ge(aT_hi, NB + n + 1)
                dve.tensor_tensor(xl[:, :, n * P:(n + 1) * P], ps[:, 7, 0:2 * P].rearrange("p (m n) -> p m n", m=2),
                                  xh[:, :, n * P:(n + 1) * P].bitcast(F32), ALU.subtract).then_inc(aT_lo, 1)
        dve.wait_ge(qbd_z, 2)
        for m in range(2):
            for e in range(2):
                ins = dve.tensor_copy(xqb[64 * e:64 * e + 64, m, :, 2 * m + e], qc[64 * e:64 * e + 64, m, S:T])
        ins.then_inc(qbd_ok, 1)
        dve.wait_ge(sl_t, 2)
        self_.link(dve.tensor_reduce(xss[:, 0:1], ps[0:32, 3, 0:NM], AX.X, ALU.max))
        dve.tensor_scalar(xss[:, 1:2], xss[:, 0:1], -DH ** -0.5, None, ALU.mult).then_inc(s_nm, 1)
        dve.wait_ge(s_exp, 2)
        self_.link(dve.reciprocal(xss[:, 3:4], xss[:, 2:3]))
        dve.tensor_scalar(xls[:, :], xls[:, :], xss[:, 3:4], None, ALU.mult).then_inc(s_p, 1)
        dve.wait_ge(sv_t, DB + DB)
        heads = ps[:, 7, 256:256 + 64].rearrange("p (m b h) -> p m b h", m=2, b=DB)
        for m in range(2):
            for e in range(2):
                ins = dve.tensor_copy(xas[64 * e:64 * e + 64, m, :], heads[64 * e:64 * e + 64, m, :, 2 * m + e])
        ins.then_inc(s_att, 1)
        dve.wait_ge(s_hi, 2)
        dve.tensor_tensor(xl[:, :, S:T], xas[:, :, :], xh[:, :, S:T].bitcast(F32), ALU.subtract).then_inc(s_lo, 1)
        norm(2, 24, lambda k: add_to_x(k, UNITS_TO[SLOT_CO] + 3 * k, 3 * (k % 2), 0))

        def conv(g, q):
            tile = up_tile(g, q)
            w = lambda j: fw[:, j, bass.ds(tile, 1)]
            e, y_ = ue[q % 2], uy[q]
            dve.wait_ge(f_c, 6 + 12 * g + 3 * q + 3)
            n0 = self_.n
            ins = dve.scalar_tensor_tensor(out=y_[:, 0:S], in0=e[:, 1:1 + S], scalar=w(1), in1=y_[:, 0:S], op0=ALU.mult, op1=ALU.add)
            ins = dve.scalar_tensor_tensor(out=y_[:, S:T], in0=cf[:, :, 1, bass.ds(tile, 1)].rearrange("p b a -> p (b a)"),
                                           scalar=w(1), in1=y_[:, S:T], op0=ALU.mult, op1=ALU.add)
            self_.link(ins)
            dve.scalar_tensor_tensor(out=y_[:, 0:S], in0=e[:, 0:S], scalar=w(0), in1=y_[:, 0:S], op0=ALU.mult, op1=ALU.add)
            dve.scalar_tensor_tensor(out=y_[:, S:T], in0=cf[:, :, 0, bass.ds(tile, 1)].rearrange("p b a -> p (b a)"),
                                     scalar=w(0), in1=y_[:, S:T], op0=ALU.mult, op1=ALU.add).then_inc(cv, 1)
            if q % 2:
                dve.wait_ge(cv, 4 * g + q + 1)
                dve.wait_ge(slu, 2 * g + q // 2 + 1)
                dve.tensor_tensor(y_[:, :], uy[q - 1][:, :], y_[:, :], ALU.mult).then_inc(prd, 1)

        def down(g, half, unit0):
            for m in range(4 * half, 4 * half + 4):
                for c in range(3):
                    n = 3 * m + c
                    cols = slice(c * CH, (c + 1) * CH)
                    dve.wait_ge(g_done, unit0 + n + 1)
                    dve.wait_ge(res_c, 6 + 48 + 24 * g + n)
                    dve.tensor_tensor(xT[:, m, cols], xT[:, m, cols], ps[:, 6 + n % 2, 0:CH], ALU.add).then_inc(res_c, 1)

        for q in range(4):
            conv(0, q)
        n0 = self_.n
        with dve.Fori(0, (NG - 1) // 2) as i:
            self_.n = n0 + 8 * i
            for e in range(2):
                g = 2 * i + e
                unit0 = FFN0 + 36 * g + 24
                for q in range(3):
                    conv(g + 1, q)
                down(g, 0, unit0)
                conv(g + 1, 3)
                down(g, 1, unit0)
        self_.n = n0 + 4 * (NG - 1)
        norm(3, 32, lambda k: down(NG - 1, k // 4, UNITS_TO[SLOTS - 2]) if k % 4 == 0 else None)
        for t in range(NB + 1):
            dve.wait_ge(yo_t, 2 * t + 2)
            if t >= 2:
                dve.wait_ge(y_out[t % 2], 16 * (t // 2))
            rows = P if t < NB else DB
            dve.tensor_copy(ytk[t % 2][0:rows, 512:1024], ps[0:rows, 4 + 2 * (t % 2), :]).then_inc(yo_d, 1)

    @block.tensor
    def _(pe):
        def tr(out, in_):
            n = in_.shape[0]
            q = in_.start_partition() if callable(in_.start_partition) else in_.start_partition
            return pe.transpose(out, in_, ident[q:q + n, q:q + n])

        def gemm(out, j, m0, m, ktiles, hi, lo, width=P):
            view = lambda w: w[j % 2][:, :].rearrange("p (k n) -> p k n", n=width)
            for k in range(ktiles):
                for q, (w, x) in enumerate(((wh, hi), (wh, lo), (wl, hi))):
                    mm = pe.matmul(out, view(w)[:, k, m0:m0 + m], x(k), start=(k == 0 and q == 0),
                                   stop=(k == ktiles - 1 and q == 2))
            return mm

        pe.wait_ge(par_in, 16 * NPAR)
        tr(ps[:, 7, 0:52], prm[:, :])
        tr(ps[:, 7, 64:64 + CW * CT], cwr[:, :]).then_inc(par_t, 1)
        for j in range(4):
            mm = tr(ps[:, 6, j * 2 * FT:(j + 1) * 2 * FT], fwr[:, j, :])
        mm.then_inc(par_t, 1)
        for b in range(DB):
            mm = tr(ps[:, 5 if b < 5 else 4, b % 5 * 88:b % 5 * 88 + 88], cfr[:, b, :])
        mm.then_inc(par_t, 1)
        pe.wait_ge(rbx_ok, 1)
        pe.wait_ge(par_c, 3)
        for h in range(NH):
            if h >= 2:
                pe.wait_ge(tp_c, h - 1)
            pe.matmul(ps[:, 5 + h % 2, 0:384], rbx[:, h, :], toep[:, :], start=True, stop=True).then_inc(tp_t, 1)
        for n in range(2 * NB + 1):
            t, g = divmod(n, 2)
            if n % 8 == 0:
                pe.wait_ge(x_in, 48)
            if n >= 3:
                pe.wait_ge(xt_c, n - 2)
            if n < 2 * NB:
                for q in range(4):
                    mm = tr(ps[:, n % 3, q * P:(q + 1) * P], xs[:, t, (4 * g + q) * P:(4 * g + q + 1) * P])
            else:
                for q in range(8):
                    mm = tr(ps[:, n % 3, q * 8:q * 8 + 8], xsm[:, q * P:(q + 1) * P])
            mm.then_inc(xt_t, 1)
        pe.wait_ge(mem_in, 16)
        pe.wait_ge(tp_c, NH)
        for n in range(4):
            t, g = divmod(n, 2)
            if n >= 2:
                pe.wait_ge(mt_c, n - 1)
            for q in range(4):
                mm = tr(ps[:, 3 + n % 2, q * P:(q + 1) * P], mtok[:, t, (4 * g + q) * P:(4 * g + q + 1) * P])
            mm.then_inc(mt_t, 1)
        pe.wait_ge(m_ss, 1)
        pe.wait_ge(ones_ok, 1)
        pe.matmul(ps[:, 7, 0:NM], ones[:, :], mr[:, :], start=True, stop=True).then_inc(m_ss, 1)
        pe.wait_ge(m_lo, 1)
        for j in range(4):
            pe.wait_ge(w_lo, j + 1)
            if j >= 2:
                pe.wait_ge(ckv_c, j - 1)
            mm = gemm(ps[:, 5 + j % 2, 0:NM], j, 0, P, KT, lambda k: mhh[:, k, :], lambda k: mhl[:, k, :])
            mm.then_inc(g_done, 1)
        pe.wait_ge(ckv_c, 4)
        for t in range(2):
            for q in range(4):
                src = kmT[:, q, t * P:(t + 1) * P] if q < 2 else mvT[:, q - 2, t * P:(t + 1) * P]
                mm = tr(ps[:, 3 + t, q * P:(q + 1) * P], src)
            mm.then_inc(mkv_t, 1)

        def norm_sum(i):
            pe.wait_ge(n_acc, KT * (i + 1))
            for c in range(3):
                mm = pe.matmul(ps[:, c, 0:CH], ones[:, :], nr[:, c * CH:(c + 1) * CH], start=True, stop=True)
            mm.then_inc(n_ss, 1)

        norm_sum(0)

        n_aux = 0

        def aux():
            nonlocal n_aux
            if n_aux >= 2:
                pe.wait_ge(aux_c, n_aux - 1)
            n_aux += 1
            return ps[:, 6 + (n_aux - 1) % 2, :]

        def in_slot(js):
            kind, m, _, cols = IN_SLOTS[js]
            j = SLOT_IN + js
            pe.wait_ge(w_lo, j + 1)
            for c in range(3):
                if js >= 2:
                    pe.wait_ge(in_c, 3 * js + c - 5)
                out = ps[0:cols, 3 * (js % 2) + c, 0:CH]
                at = slice(c * CH, (c + 1) * CH)
                gemm(out, j, 0, cols, KT, lambda k: hh[:, k, at], lambda k: hl[:, k, at]).then_inc(g_done, 1)

        def tokens(src):
            for g in range(2):
                bank = aux()
                for q in range(4):
                    t = 4 * g + q
                    mm = tr(bank[:, q * P:q * P + src.shape[0]], src[:, t * P:(t + 1) * P])
                mm.then_inc(aux_t, 1)
            tr(aux()[0:DB, 0:src.shape[0]], src[:, S:T]).then_inc(aux_t, 1)

        pe.wait_ge(mkv_c, 4)
        pe.wait_ge(n_lo, KT)
        pe.wait_ge(n_var, 1)
        for kind, i in order_of_w_in():
            if kind == "slot":
                in_slot(i)
            elif kind == "ki":
                pe.wait_ge(in_c, 15)
                tokens(kw[:, :])
            elif kind == "idx":
                if i == 2:
                    pe.wait_ge(ki_dup, 16)
                for b, h, f, w in IDX_UNITS:
                    if b == i:
                        lo = 64 * (h % 2)
                        keys = (ki2 if h % 2 else kw)[lo:lo + DH, 512 * f:512 * f + w]
                        pe.matmul(aux()[:, 0:w], qx[lo:lo + DH, h // 2, b * P:(b + 1) * P], keys,
                                  start=True, stop=True).then_inc(aux_t, 1)
            elif kind == "ktok":
                pe.wait_ge(in_c, 3 * (5 + i) + 3)
                tokens(kT_[:, i, :])
            elif kind == "vtok":
                pe.wait_ge(in_c, 3 * (9 + i) + 3)
                tokens(vT1[:, :])
            else:
                pe.wait_ge(u_ok, 12)
                bank = aux()
                for m in range(CT):
                    mm = tr(bank[0:HALO, m * P:(m + 1) * P], u[:, m, S:S + HALO])
                mm.then_inc(aux_t, 1)
                bank = aux()
                for m in range(CT):
                    mm = tr(bank[0:DB, m * P:(m + 1) * P], us[:, m, :, HALO])
                mm.then_inc(aux_t, 1)
                pe.wait_ge(cc_in, 16)
                for g in range(2):
                    bank = aux()
                    for m in range(CT):
                        mm = tr(bank[:, m * 120:(m + 1) * 120], ccr[:, g, m * P:(m + 1) * P])
                    mm.then_inc(aux_t, 1)

        pe.wait_ge(tap, CT * CW)
        pe.wait_ge(y_ok, 1)
        for c in range(3):
            for m in range(CT):
                mm = pe.matmul(ps[:, c, 0:CH], ones[:, :], y[:, m, c * CH:(c + 1) * CH], start=(m == 0), stop=(m == CT - 1))
        mm.then_inc(ln_s, 1)
        for m in range(CT):
            pe.wait_ge(ln_sq, m + 1)
            for c in range(3):
                mm = pe.matmul(ps[:, 3 + c, 0:CH], ones[:, :], lq[m % 2][:, c * CH:(c + 1) * CH], start=(m == 0), stop=(m == CT - 1))
            mm.then_inc(ln_ss, 1)
        pe.wait_ge(ln_var, 1)
        pe.wait_ge(aux_c, AUX_IN)
        for i in range(len(ITEMS) + 13):
            if i < len(ITEMS):
                b, h = ITEMS[i]
                ext, lo = P * (b + 1), 64 * (h % 2)
                if i >= 2:
                    pe.wait_ge(added, i - 1)
                for f in range(0, ext, 512):
                    w = min(512, ext - f)
                    mm = pe.matmul(pair(i)[:, f:f + w], qx[lo:lo + DH, h // 2, b * P:(b + 1) * P],
                                   kT_[lo:lo + DH, h // 2, f:f + w], start=True, stop=True)
                mm.then_inc(qk, 1)
            if 2 <= i < len(ITEMS) + 2:
                n = i - 2
                b = ITEMS[n][0]
                pe.wait_ge(exp_ok, n + 1)
                if n >= 1:
                    pe.wait_ge(t0_c, n)
                for k in range(min(b + 1, 4)):
                    mm = tr(ps[:, 4, k * P:(k + 1) * P], lg[n % 2][:, k * P:(k + 1) * P])
                mm.then_inc(t0_t, 1)
                if b >= 4:
                    if late(n):
                        pe.wait_ge(t1_c, late(n))
                    for k in range(4, b + 1):
                        mm = tr(ps[:, 5, (k - 4) * P:(k - 3) * P], lg[n % 2][:, k * P:(k + 1) * P])
                    mm.then_inc(t1_t, 1)
            if 3 <= i < len(ITEMS) + 3:
                n = i - 3
                b, h = ITEMS[n]
                if n == 0:
                    pe.wait_ge(v_in, 16)
                pe.wait_ge(t0_c, n + 1)
                if b >= 4:
                    pe.wait_ge(t1_c, late(n + 1))
                if h == 0 and b >= 1:
                    pe.wait_ge(att_ok, b)
                for k in range(b + 1):
                    mm = pe.matmul(ps[:, 6, h * DH:(h + 1) * DH], pt[n % 2][:, k, :], v_[:, k, h * DH:(h + 1) * DH],
                                   start=(k == 0), stop=(k == b))
                mm.then_inc(pv, 1)
            if i >= 12 and (i - 12) % 8 == 0 and (i - 12) // 8 < NB:
                b = (i - 12) // 8
                pe.wait_ge(att_ok, b + 1)
                if b >= 1:
                    pe.wait_ge(aT_lo, b)
                for m in range(CT):
                    mm = tr(ps[:, 7, m * P:(m + 1) * P], att[:, m * P:(m + 1) * P])
                mm.then_inc(aT_t, 1)

        pe.wait_ge(aT_lo, NB)
        pe.wait_ge(kip_in, 16 * DB * NPG)
        pe.wait_ge(wsel_ok, 2)

        def combine(n):
            pe.wait_ge(si_r, n + 1)
            pe.matmul(ps[0:DB, 5, :], wsel[:, n, :], rsm[n % 2][:, 0:PAST], start=(n == 0), stop=(n == DB - 1))
            pe.matmul(ps[0:DB, 6, 0:1], wsel[:, n, :], rsm[n % 2][:, PAST:KEYS], start=(n == 0), stop=(n == DB - 1)).then_inc(si_w, 1)

        for b in range(DB):
            if b >= 2:
                pe.wait_ge(si_c, b - 1)
            for q in range(NPG):
                mm = tr(ps[0:DH, b % 2, q * P:(q + 1) * P], kip[:, NPG * b + q, :])
            mm.then_inc(si_t, 1)
            pe.wait_ge(si_c, b + 1)
            if b >= 2:
                pe.wait_ge(si_r, b - 1)
            pe.matmul(ps[0:NH, 2 + b % 2, :], qis[:, b, :], kis[b % 2][:, :], start=True, stop=True)
            pe.matmul(ps[0:NH, 4 + 3 * (b % 2), 0:1], qis[:, b, :], kws[0:DH, b:b + 1], start=True, stop=True).then_inc(si_s, 1)
            if b >= 1:
                combine(b - 1)
        combine(DB - 1)
        pe.wait_ge(qbd_ok, 1)
        for n in range(DB * NPG + 1):
            if n < DB * NPG:
                pe.wait_ge(kp_in[n % 4], 16 * (n // 4 + 1))
                if n >= 2:
                    pe.wait_ge(sk_c, n - 1)
                for m in range(CT):
                    mm = tr(ps[:, n % 2, m * P:(m + 1) * P], kpg[n % 4][:, m * P:(m + 1) * P])
                mm.then_inc(sk_t, 1)
            if n >= 1:
                b, q = divmod(n - 1, NPG)
                pe.wait_ge(sk_c, n)
                for m in range(CT):
                    mm = pe.matmul(ps[:, 7, q * 64 + b * 8:q * 64 + b * 8 + 8], kpt[(n - 1) % 2][:, m, :], qbd[:, m, b, :],
                                   start=(m == 0), stop=(m == CT - 1))
                mm.then_inc(sk_s, 1)
        for m in range(CT):
            pe.matmul(ps[0:64, 3, 0:8], qbd[:, m, :, :].rearrange("p b h -> p (b h)"), kT_[:, m, S:T], start=(m == 0), stop=(m == CT - 1))
        pe.wait_ge(sl_c, 1)
        for q in range(NPG):
            mm = tr(ps[0:64, 4, q * P:(q + 1) * P], sl[:, q, :])
        mm.then_inc(sl_t, 1)
        pe.wait_ge(smask, 1)
        pe.wait_ge(srb_ok, 1)
        rel = srb[:, :, :].rearrange("r b h -> r (b h)")
        for bank, k0, k1 in ((5, 0, PAST), (6, PAST, KEYS)):
            pe.matmul(ps[0:64, bank, 0:k1 - k0], sameT[:, :], ssc[:, k0:k1], start=True, stop=False)
            mm = pe.matmul(ps[0:64, bank, 0:k1 - k0], rel, samp[:, k0:k1], start=False, stop=True)
        mm.then_inc(sb_t, 1)
        pe.wait_ge(s_p, 1)
        for q in range(NPG):
            tr(ps[:, 0, q * 64:q * 64 + 64], ls[:, q * P:(q + 1) * P])
        tr(ps[0:8, 1, 0:64], pd[:, :]).then_inc(sp_t, 1)
        pe.wait_ge(sp_c, 1)
        for b in range(DB):
            pe.wait_ge(vp_in[b % 2], 64 * (b // 2 + 1))
            for m in range(CT):
                out = ps[:, 7, 256 + (m * DB + b) * 8:256 + (m * DB + b) * 8 + 8]
                for q in range(NPG):
                    pe.matmul(out, vpg[b % 2][:, q, m * P:(m + 1) * P], spT[:, q, b * 8:b * 8 + 8], start=(q == 0), stop=False)
                mm = pe.matmul(out, ksm[:, 1, m * P:(m + 1) * P], pdT[:, b * 8:b * 8 + 8], start=False, stop=True)
            mm.then_inc(sv_t, 1)

        pe.wait_ge(s_lo, 1)
        pe.wait_ge(ln_lo, CT)
        with pe.Fori(0, 4) as i:
            for q in range(2):
                pe.wait_ge(w_lo, 2 * i + (SLOT_O + q + 1))
                for c in range(3):
                    at = slice(c * CH, (c + 1) * CH)
                    pe.wait_ge(res_c, 6 * i + (3 * q + c + 1))
                    gemm(ps[:, 3 * q + c, 0:CH], SLOT_O + q, 0, P, KT, lambda k: hh[:, k, at], lambda k: hl[:, k, at]).then_inc(g_done, 1)
        norm_sum(1)
        pe.wait_ge(n_lo, 2 * KT)
        for n in range(6):
            m, c = divmod(n, 3)
            at = slice(c * CH, (c + 1) * CH)
            pe.wait_ge(w_lo, SLOT_CQ + m + 1)
            gemm(ps[:, n, 0:CH], SLOT_CQ + m, 0, P, KT, lambda k: hh[:, k, at], lambda k: hl[:, k, at]).then_inc(g_done, 1)
        pe.wait_ge(qc_c, 6)
        for i in range(NB + 2):
            if i < NB:
                if i >= 2:
                    pe.wait_ge(exp_ok, N_ITEMS + i - 1)
                for h in range(MH):
                    lo = 64 * (h % 2)
                    mm = pe.matmul(ps[:, 2 * (i % 2) + h % 2, h // 2 * NM:(h // 2 + 1) * NM], qc[lo:lo + DH, h // 2, i * P:(i + 1) * P],
                                   kmT[lo:lo + DH, h // 2, :], start=True, stop=True)
                mm.then_inc(qk, 1)
            if 1 <= i < NB + 1:
                n = i - 1
                pe.wait_ge(exp_ok, N_ITEMS + n + 1)
                if n >= 1:
                    pe.wait_ge(t0_c, N_ITEMS + n)
                    pe.wait_ge(t1_c, N_LATE + n)
                for k in range(8):
                    mm = tr(ps[:, 4 + k // 4, k % 4 * P:(k % 4 + 1) * P], xp[n % 2][:, k // 2, k % 2 * P:(k % 2 + 1) * P])
                    if k % 4 == 3:
                        mm.then_inc(t1_t if k == 7 else t0_t, 1)
                pe.wait_ge(t0_c, N_ITEMS + n + 1)
                pe.wait_ge(t1_c, N_LATE + n + 1)
                if n >= 1:
                    pe.wait_ge(att_ok, NB + n)
                for h in range(MH):
                    for t in range(2):
                        mm = pe.matmul(ps[:, 6, h * DH:(h + 1) * DH], xpt[n % 2][:, 2 * h + t, :], vm[:, t, h * DH:(h + 1) * DH],
                                       start=(t == 0), stop=(t == 1))
                mm.then_inc(pv, 1)
            if i >= 2:
                n = i - 2
                pe.wait_ge(att_ok, NB + n + 1)
                if n >= 1:
                    pe.wait_ge(aT_lo, NB + n)
                for m in range(2):
                    mm = tr(ps[:, 7, m * P:(m + 1) * P], xa[:, m * P:(m + 1) * P])
                mm.then_inc(aT_t, 1)
        pe.wait_ge(aT_lo, NB + NB)
        pe.wait_ge(qbd_ok, 2)
        for b in range(DB + 1):
            if b < DB:
                pe.wait_ge(xk_in[b % 2], 16 * (b // 2 + 1))
                if b >= 2:
                    pe.wait_ge(sk_c, N_PAGES + b - 1)
                for k in range(4):
                    mm = tr(ps[:, b % 2, k * P:(k + 1) * P], xkp[b % 2][:, k // 2, k % 2 * P:(k % 2 + 1) * P])
                mm.then_inc(sk_t, 1)
            if b >= 1:
                n = b - 1
                pe.wait_ge(sk_c, N_PAGES + n + 1)
                for t in range(2):
                    for m in range(2):
                        mm = pe.matmul(ps[:, 2, t * 32 + n * MH:t * 32 + (n + 1) * MH], xkt[n % 2][:, t, m, :], xqb[:, m, n, :],
                                       start=(m == 0), stop=(m == 1))
                mm.then_inc(sk_s, 1)
        pe.wait_ge(sl_c, 2)
        for t in range(2):
            mm = tr(ps[0:32, 3, t * P:(t + 1) * P], xsl[:, t, :])
        mm.then_inc(sl_t, 1)
        pe.wait_ge(s_p, 2)
        for t in range(2):
            mm = tr(ps[:, 4, t * 32:(t + 1) * 32], xls[:, t * P:(t + 1) * P])
        mm.then_inc(sp_t, 1)
        pe.wait_ge(sp_c, 2)
        for b in range(DB):
            pe.wait_ge(xv_in[b % 2], 16 * (b // 2 + 1))
            for m in range(2):
                for t in range(2):
                    mm = pe.matmul(ps[:, 7, 256 + (m * DB + b) * MH:256 + (m * DB + b + 1) * MH], xvp[b % 2][:, t, m * P:(m + 1) * P],
                                   xsp[:, t, b * MH:(b + 1) * MH], start=(t == 0), stop=(t == 1))
            mm.then_inc(sv_t, 1)
        pe.wait_ge(s_lo, 2)
        for n in range(24):
            m, c = divmod(n, 3)
            at = slice(c * CH, (c + 1) * CH)
            pe.wait_ge(w_lo, SLOT_CO + m // 4 + 1)
            pe.wait_ge(res_c, 24 + n + 1)
            gemm(ps[:, n % 6, 0:CH], SLOT_CO + m // 4, m % 4 * P, P, 2, lambda k: xh[:, k, at], lambda k: xl[:, k, at], 512).then_inc(g_done, 1)
        norm_sum(2)

        def up(g, slot0):
            for q in range(4):
                pe.wait_ge(w_lo, slot0 + (q + 1))
                for c in range(3):
                    at = slice(c * CH, (c + 1) * CH)
                    pe.wait_ge(f_c, 12 * g + (3 * q + c + 1))
                    gemm(ps[:, 3 * (q % 2) + c, 0:CH], SLOT_F + q, 0, P, KT, lambda k: hh[:, k, at], lambda k: hl[:, k, at]).then_inc(g_done, 1)

        def down(g, slot0, e):
            pe.wait_ge(glo, 2 * g + 2)
            for n in range(24):
                m, c = divmod(n, 3)
                at = slice(c * CH, (c + 1) * CH)
                if n % 12 == 0:
                    pe.wait_ge(w_lo, slot0 + (m // 4 + 1))
                pe.wait_ge(res_c, 24 * g + (6 + 48 - 1 + n))
                gemm(ps[:, 6 + n % 2, 0:CH], SLOT_F + m // 4, m % 4 * P, P, 2, lambda k: gh[e][:, k, at], lambda k: gl[e][:, k, at], 512).then_inc(g_done, 1)

        pe.wait_ge(n_lo, 3 * KT)
        pe.wait_ge(n_var, 3)
        up(0, SLOT_F)
        with pe.Fori(0, (NG - 1) // 2) as i:
            for e in range(2):
                g = 2 * i + e
                up(g + 1, 6 * g + (SLOT_F + 4))
                down(g, 6 * g + (SLOT_F + 8), e)
        down(NG - 1, SLOTS - 2, (NG - 1) % 2)
        pe.wait_ge(f_c, 6 + 12 * NG)
        for q in range(5):
            mm = tr(ps[0:88, 3 + q // 4, q % 4 * P:(q % 4 + 1) * P], upl[:, 2 * q:2 * q + 2, :].rearrange("p r c -> p (r c)"))
            if q >= 3:
                mm.then_inc(fo_t, 1)
        norm_sum(3)
        pe.wait_ge(fo_c, 2)
        pe.wait_ge(n_h, 4 * KT)
        for t in range(NB + 1):
            cols = slice(t * P, (t + 1) * P) if t < NB else slice(S, T)
            rows = P if t < NB else DB
            if t >= 2:
                pe.wait_ge(yo_a, t - 1)
                pe.wait_ge(yo_d, t - 1)
            for k in range(KT):
                mm = tr(ps[0:rows, 3 + 2 * (t % 2) + k // 4, k % 4 * P:(k % 4 + 1) * P], yT[:, k, cols])
                if k % 4 == 3:
                    mm.then_inc(yo_t, 1)

    ctx.close()


_INS = ["x_prompt", "x_sample", "mem_prompt", "cache_k", "cache_v", "cache_idx_k", "page_table", "cache_conv",
        "cache_ffn", "cache_mem_k", "cache_mem_v", "rel_bias", "norm_mix", "w_in", "conv_dw", "conv_db",
        "conv_ln_g", "conv_ln_b", "w_o", "norm_mem_q", "norm_mem_kv", "w_cq", "w_ckv", "w_co", "norm_ffn",
        "w_up", "ffn_dw", "ffn_db", "w_down", "norm_final"]
_OUTS = [("y_prompt", (1, S, D)), ("y_sample", (DB, 1, D)), ("k_prompt", (1, 1, S, NH, DH)),
         ("v_prompt", (1, 1, S, NH, DH)), ("idx_k_prompt", (1, 1, S, DH)), ("k_sample", (1, DB, 1, NH, DH)),
         ("v_sample", (1, DB, 1, NH, DH)), ("idx_k_sample", (1, DB, 1, DH)), ("conv_prompt", (1, 1, HALO, 512)),
         ("conv_sample", (1, DB, HALO, 512)), ("ffn_prompt", (1, 1, 2, 2 * DFF)), ("ffn_sample", (1, DB, 2, 2 * DFF)),
         ("mem_k_prompt", (1, 1, NM, MH, DH)), ("mem_v_prompt", (1, 1, NM, MH, DH))]


def kernel(**inputs):
    import concourse.bacc as _bacc
    from concourse.bass_utils import run_bass_kernel_spmd as _run

    nc = _bacc.Bacc("TRN2", target_bir_lowering=False, num_devices=1)
    arrays, a, o = {}, {}, {}
    for name, x in [(n, inputs[n]) for n in _INS] + sorted(constants().items()):
        x = np.ascontiguousarray(x)
        arrays[f"in_{name}"] = x
        a[name] = nc.dram_tensor(f"in_{name}", x.shape, mybir.dt.from_np(x.dtype), kind="ExternalInput").ap()
    for name, shape in _OUTS:
        o[name] = nc.dram_tensor(f"out_{name}", shape, F32, kind="ExternalOutput").ap()
    build(nc, a, o)
    r = _run(nc, [arrays], core_ids=[0])
    return tuple(r.results[0][f"out_{name}"] for name, _ in _OUTS)
```
